# Optimizing a Trainium2 kernel written in Bass

```python
import math
import jax, jax.numpy as jnp
from jax import lax
import numpy as np

D_MODEL = 1024
BATCH = 1
SEQ = 1024
DEPTH = 1
DEC_BATCH = 8
DEC_SEQ = 1
PAST_LEN = 2048
PAGE_SIZE = 128

HEAD_DIM = 64
N_HEADS = D_MODEL // HEAD_DIM
NSA_HEADS = N_HEADS // 2
RET_HEADS = N_HEADS - NSA_HEADS
KV_GROUPS = 2
HPG = NSA_HEADS // KV_GROUPS
CMP_BLK = 32
CMP_STRIDE = 16
CMP_HID = 4 * HEAD_DIM
SEL_BLK = 64
SEL_TOPN = 16
WINDOW = 512
Q_BLK = 128
RET_CHUNK = 128
D_FF = ((8 * D_MODEL + 3 * 256 - 1) // (3 * 256)) * 256
NSA_W = NSA_HEADS * HEAD_DIM
KV_W = KV_GROUPS * HEAD_DIM
GATE_W = NSA_HEADS * 3
RET_W = RET_HEADS * HEAD_DIM
IN_COLS = NSA_W + 6 * KV_W + GATE_W + 4 * RET_W
SPLITS = [NSA_W, NSA_W + 6 * KV_W, NSA_W + 6 * KV_W + GATE_W,
          NSA_W + 6 * KV_W + GATE_W + RET_W, NSA_W + 6 * KV_W + GATE_W + 2 * RET_W,
          NSA_W + 6 * KV_W + GATE_W + 3 * RET_W]
ROPE_THETA = 10000.0
RMS_EPS = 1e-6

kernel_name = 'hybrid_nsa_retention_decode_step'

def rmsnorm(x, g):
    xf = x.astype(jnp.float32)
    y = xf * lax.rsqrt(jnp.mean(xf * xf, axis=-1, keepdims=True) + RMS_EPS)
    return (y * g.astype(jnp.float32)).astype(x.dtype)

def rope(x, pos):
    half = HEAD_DIM // 2
    inv = 1.0 / (ROPE_THETA ** (jnp.arange(half, dtype=jnp.float32) / half))
    ang = pos.astype(jnp.float32)[:, None] * inv[None, :]
    cos = jnp.cos(ang)[:, None, :]
    sin = jnp.sin(ang)[:, None, :]
    xf = x.astype(jnp.float32)
    x1, x2 = xf[..., :half], xf[..., half:]
    return jnp.concatenate([x1 * cos - x2 * sin, x2 * cos + x1 * sin], axis=-1).astype(x.dtype)

def masked_softmax(s, mask):
    s = jnp.where(mask, s, -jnp.inf)
    m = jnp.max(s, axis=-1, keepdims=True)
    m = jnp.where(jnp.isfinite(m), m, 0.0)
    e = jnp.where(mask, jnp.exp(s - m), 0.0)
    return e / jnp.maximum(jnp.sum(e, axis=-1, keepdims=True), 1e-30)

def project(h, w_in, pos):
    B, T, _ = h.shape
    p = h @ w_in
    q, kv, gt, rq, rk, rv, rg = jnp.split(p, SPLITS, axis=-1)
    q = rope(q.reshape(B, T, NSA_HEADS, HEAD_DIM), pos)
    kv = kv.reshape(B, T, 3, 2, KV_GROUPS, HEAD_DIM)
    k = rope(kv[:, :, :, 0].reshape(B, T, 3 * KV_GROUPS, HEAD_DIM), pos).reshape(B, T, 3, KV_GROUPS, HEAD_DIM)
    v = kv[:, :, :, 1]
    rows = jnp.stack([k[:, :, 0], v[:, :, 0], k[:, :, 1], v[:, :, 1]], axis=2)
    win = jnp.stack([k[:, :, 2], v[:, :, 2]], axis=2)
    gates = jax.nn.sigmoid(gt.reshape(B, T, NSA_HEADS, 3))
    hs = (B, T, RET_HEADS, HEAD_DIM)
    rq = rope(rq.reshape(hs), pos)
    rk = rope(rk.reshape(hs), pos) * (HEAD_DIM ** -0.5)
    return q, gates, rows, win, rq, rk, rv.reshape(hs), rg.reshape(hs)

def compress(rows, pos_emb, w1, w2):
    L = rows.shape[0]
    nb = (L - CMP_BLK) // CMP_STRIDE + 1
    idx = np.arange(nb)[:, None] * CMP_STRIDE + np.arange(CMP_BLK)[None, :]
    blk = rows[idx] + pos_emb[None, :, None, :]
    blk = blk.transpose(0, 2, 1, 3).reshape(nb, KV_GROUPS, CMP_BLK * HEAD_DIM)
    return jax.nn.gelu(blk @ w1) @ w2

def block_cover(L):
    nb = (L - CMP_BLK) // CMP_STRIDE + 1
    nsel = -(-L // SEL_BLK)
    c0 = np.arange(nb) * CMP_STRIDE
    s0 = np.arange(nsel) * SEL_BLK
    m = (c0[None, :] < s0[:, None] + SEL_BLK) & (c0[None, :] + CMP_BLK > s0[:, None])
    return jnp.asarray(m.astype(np.float32))

def nsa_queries(q, gates, q_pos, kcb, vcb, cover, ks, vs, kw, vw, w_pos):
    Sq = q.shape[0]
    L = ks.shape[0]
    scale = HEAD_DIM ** -0.5
    qg = q.reshape(Sq, KV_GROUPS, HPG, HEAD_DIM)
    nb = kcb.shape[0]
    blk_end = jnp.asarray(np.arange(nb) * CMP_STRIDE + CMP_BLK - 1, jnp.int32)
    s_c = jnp.einsum('sghd,ngd->sghn', qg, kcb).astype(jnp.float32) * scale
    p_c = masked_softmax(s_c, (blk_end[None, :] <= q_pos[:, None])[:, None, None, :])
    o_c = jnp.einsum('sghn,ngd->sghd', p_c.astype(vcb.dtype), vcb)
    imp = jnp.einsum('sghn,jn->sgj', p_c, cover)
    nsel = cover.shape[0]
    j = jnp.arange(nsel)[None, :]
    cur = (q_pos // SEL_BLK)[:, None]
    forced = (j == 0) | (j == cur) | (j == cur - 1)
    valid = j * SEL_BLK <= q_pos[:, None]
    score = jnp.where(forced[:, None], jnp.inf, jnp.where(valid[:, None], imp, -jnp.inf))
    n_top = min(SEL_TOPN, nsel)
    _, idx = lax.top_k(score, n_top)
    tok = (idx[..., None] * SEL_BLK + jnp.arange(SEL_BLK)).reshape(Sq, KV_GROUPS, n_top * SEL_BLK)
    tok_c = jnp.minimum(tok, L - 1)
    g_idx = jnp.arange(KV_GROUPS)[None, :, None]
    k_g = ks[tok_c, g_idx]
    v_g = vs[tok_c, g_idx]
    s_s = jnp.einsum('sghd,sgkd->sghk', qg, k_g).astype(jnp.float32) * scale
    p_s = masked_softmax(s_s, (tok <= q_pos[:, None, None])[:, :, None, :])
    o_s = jnp.einsum('sghk,sgkd->sghd', p_s.astype(v_g.dtype), v_g)
    wmask = (w_pos[None, :] <= q_pos[:, None]) & (w_pos[None, :] > q_pos[:, None] - WINDOW) & (w_pos[None, :] >= 0)
    s_w = jnp.einsum('sghd,wgd->sghw', qg, kw).astype(jnp.float32) * scale
    p_w = masked_softmax(s_w, wmask[:, None, None, :])
    o_w = jnp.einsum('sghw,wgd->sghd', p_w.astype(vw.dtype), vw)
    g = gates.reshape(Sq, KV_GROUPS, HPG, 3).astype(o_c.dtype)
    o = g[..., 0:1] * o_c + g[..., 1:2] * o_s + g[..., 2:3] * o_w
    return o.reshape(Sq, NSA_W)

def nsa_prompt_seq(q, gt, rows, win, cw):
    pk, w1k, w2k, pv, w1v, w2v = cw
    L = q.shape[0]
    kcb = compress(rows[:, 0], pk, w1k, w2k)
    vcb = compress(rows[:, 1], pv, w1v, w2v)
    cover = block_cover(L)
    win_pad = jnp.concatenate([jnp.zeros((WINDOW,) + win.shape[1:], win.dtype), win], axis=0)

    def qblock(i):
        start = i * Q_BLK
        qb = lax.dynamic_slice_in_dim(q, start, Q_BLK, 0)
        gb = lax.dynamic_slice_in_dim(gt, start, Q_BLK, 0)
        wb = lax.dynamic_slice_in_dim(win_pad, start, WINDOW + Q_BLK, 0)
        q_pos = start + jnp.arange(Q_BLK)
        w_pos = start - WINDOW + jnp.arange(WINDOW + Q_BLK)
        return nsa_queries(qb, gb, q_pos, kcb, vcb, cover, rows[:, 2], rows[:, 3], wb[:, 0], wb[:, 1], w_pos)

    return lax.map(qblock, jnp.arange(L // Q_BLK)).reshape(L, NSA_W)

def nsa_sample_seq(q, gt, rows, win_cat, pages, pool, q_pos, w_pos, cw):
    pk, w1k, w2k, pv, w1v, w2v = cw
    past = pool[pages]
    past = past.reshape((-1,) + past.shape[2:])
    full = jnp.concatenate([past, rows], axis=0)
    kcb = compress(full[:, 0], pk, w1k, w2k)
    vcb = compress(full[:, 1], pv, w1v, w2v)
    cover = block_cover(full.shape[0])
    return nsa_queries(q, gt, q_pos, kcb, vcb, cover, full[:, 2], full[:, 3], win_cat[:, 0], win_cat[:, 1], w_pos)

def log_gamma():
    return jnp.log(1.0 - 2.0 ** (-5.0 - jnp.arange(RET_HEADS, dtype=jnp.float32)))

def retention_chunk(state, q, k, v, lg):
    C = q.shape[1]
    i = jnp.arange(C, dtype=jnp.float32)
    diff = i[:, None] - i[None, :]
    causal = diff >= 0
    decay = jnp.where(causal[None], jnp.exp(jnp.where(causal, diff, 0.0)[None] * lg[:, None, None]), 0.0)
    att = jnp.einsum('bihd,bjhd->bhij', q, k) * decay[None]
    o = jnp.einsum('bhij,bjhe->bihe', att, v)
    o = o + jnp.einsum('bihd,bhde->bihe', q, state) * jnp.exp((i + 1.0)[:, None] * lg[None, :])[None, :, :, None]
    k_dec = k * jnp.exp((C - 1.0 - i)[:, None] * lg[None, :])[None, :, :, None]
    state = state * jnp.exp(C * lg)[None, :, None, None] + jnp.einsum('bjhd,bjhe->bhde', k_dec, v)
    return state, o

def retention_prompt(q, k, v, lg):
    B, T, H, d = q.shape
    n = T // RET_CHUNK

    def to_chunks(a):
        return a.reshape(B, n, RET_CHUNK, H, d).transpose(1, 0, 2, 3, 4)

    s0 = jnp.zeros((B, H, d, d), jnp.float32)
    state, o = lax.scan(lambda s, c: retention_chunk(s, c[0], c[1], c[2], lg), s0,
                        (to_chunks(q), to_chunks(k), to_chunks(v)))
    return state, o.transpose(1, 0, 2, 3, 4).reshape(B, T, H, d)

def retention_out(o, g, dtype):
    o = o * lax.rsqrt(jnp.mean(o * o, axis=-1, keepdims=True) + RMS_EPS)
    o = o * jax.nn.silu(g.astype(jnp.float32))
    B, T = o.shape[:2]
    return o.reshape(B, T, RET_W).astype(dtype)

def swiglu(h, wg, wu, wd):
    return (jax.nn.silu(h @ wg) * (h @ wu)) @ wd

def setup_inputs(seed: int = 0) -> dict:
    key = jax.random.key(seed)
    ks = jax.random.split(key, 24)
    n_pages = PAST_LEN // PAGE_SIZE
    n_pool = (DEC_BATCH * n_pages * 5) // 4
    wbuf = min(WINDOW, PAST_LEN)
    f32 = jnp.float32

    def nrm(k, shape, s=1.0):
        return jax.random.normal(k, shape, f32) * s

    page_table = jax.random.permutation(ks[5], n_pool)[: DEC_BATCH * n_pages].reshape(DEC_BATCH, n_pages).astype(jnp.int32)
    return {
        'x_prompt': nrm(ks[0], (BATCH, SEQ, D_MODEL)),
        'x_sample': nrm(ks[1], (DEC_BATCH, DEC_SEQ, D_MODEL)),
        'cache_kv': nrm(ks[2], (DEPTH, n_pool, PAGE_SIZE, 4, KV_GROUPS, HEAD_DIM)),
        'cache_win': nrm(ks[3], (DEPTH, DEC_BATCH, wbuf, 2, KV_GROUPS, HEAD_DIM)),
        'state_ret': nrm(ks[4], (DEPTH, DEC_BATCH, RET_HEADS, HEAD_DIM, HEAD_DIM)),
        'page_table': page_table,
        'ln1': 1.0 + nrm(ks[6], (DEPTH, D_MODEL), 0.02),
        'w_in': nrm(ks[7], (DEPTH, D_MODEL, IN_COLS), D_MODEL ** -0.5),
        'cmp_pos_k': nrm(ks[8], (DEPTH, CMP_BLK, HEAD_DIM), 0.1),
        'cmp_w1_k': nrm(ks[9], (DEPTH, CMP_BLK * HEAD_DIM, CMP_HID), (CMP_BLK * HEAD_DIM) ** -0.5),
        'cmp_w2_k': nrm(ks[10], (DEPTH, CMP_HID, HEAD_DIM), CMP_HID ** -0.5),
        'cmp_pos_v': nrm(ks[11], (DEPTH, CMP_BLK, HEAD_DIM), 0.1),
        'cmp_w1_v': nrm(ks[12], (DEPTH, CMP_BLK * HEAD_DIM, CMP_HID), (CMP_BLK * HEAD_DIM) ** -0.5),
        'cmp_w2_v': nrm(ks[13], (DEPTH, CMP_HID, HEAD_DIM), CMP_HID ** -0.5),
        'w_out': nrm(ks[14], (DEPTH, D_MODEL, D_MODEL), D_MODEL ** -0.5),
        'ln2': 1.0 + nrm(ks[15], (DEPTH, D_MODEL), 0.02),
        'w_gate': nrm(ks[16], (DEPTH, D_MODEL, D_FF), D_MODEL ** -0.5),
        'w_up': nrm(ks[17], (DEPTH, D_MODEL, D_FF), D_MODEL ** -0.5),
        'w_down': nrm(ks[18], (DEPTH, D_FF, D_MODEL), D_FF ** -0.5),
        'ln_f': 1.0 + nrm(ks[19], (D_MODEL,), 0.02),
    }

def reference(x_prompt, x_sample, cache_kv, cache_win, state_ret, page_table, ln1, w_in,
              cmp_pos_k, cmp_w1_k, cmp_w2_k, cmp_pos_v, cmp_w1_v, cmp_w2_v, w_out, ln2,
              w_gate, w_up, w_down, ln_f):
    f32 = jnp.float32
    lg = log_gamma()
    past_len = page_table.shape[1] * PAGE_SIZE
    s_p = x_prompt.shape[1]
    s_s = x_sample.shape[1]
    pos_p = jnp.arange(s_p)
    pos_s = past_len + jnp.arange(s_s)
    win_keep = min(WINDOW, s_p)
    wbuf = cache_win.shape[2]
    w_pos_s = past_len - wbuf + jnp.arange(wbuf + s_s)
    xp, xs = x_prompt, x_sample
    kv_p, kv_s, win_p, win_s, ret_p, ret_s = [], [], [], [], [], []
    for l in range(DEPTH):
        cw = (cmp_pos_k[l], cmp_w1_k[l], cmp_w2_k[l], cmp_pos_v[l], cmp_w1_v[l], cmp_w2_v[l])
        hp = rmsnorm(xp, ln1[l])
        q, gt, rows, win, rq, rk, rv, rg = project(hp, w_in[l], pos_p)
        o_nsa = lax.map(lambda a: nsa_prompt_seq(a[0], a[1], a[2], a[3], cw), (q, gt, rows, win))
        st, o_r = retention_prompt(rq.astype(f32), rk.astype(f32), rv.astype(f32), lg)
        mix = jnp.concatenate([o_nsa, retention_out(o_r, rg, xp.dtype)], axis=-1) @ w_out[l]
        xp = xp + mix
        xp = xp + swiglu(rmsnorm(xp, ln2[l]), w_gate[l], w_up[l], w_down[l])
        kv_p.append(rows)
        win_p.append(win[:, s_p - win_keep:])
        ret_p.append(st.astype(x_prompt.dtype))
        hs = rmsnorm(xs, ln1[l])
        q, gt, rows, win, rq, rk, rv, rg = project(hs, w_in[l], pos_s)
        pool = cache_kv[l]
        win_cat = jnp.concatenate([cache_win[l], win], axis=1)
        o_nsa = lax.map(lambda a: nsa_sample_seq(a[0], a[1], a[2], a[3], a[4], pool, pos_s, w_pos_s, cw),
                        (q, gt, rows, win_cat, page_table))
        st, o_r = retention_chunk(state_ret[l].astype(f32), rq.astype(f32), rk.astype(f32), rv.astype(f32), lg)
        mix = jnp.concatenate([o_nsa, retention_out(o_r, rg, xs.dtype)], axis=-1) @ w_out[l]
        xs = xs + mix
        xs = xs + swiglu(rmsnorm(xs, ln2[l]), w_gate[l], w_up[l], w_down[l])
        kv_s.append(rows)
        win_s.append(win_cat[:, s_s:])
        ret_s.append(st.astype(state_ret.dtype))
    y_prompt = rmsnorm(xp, ln_f)
    y_sample = rmsnorm(xs, ln_f)
    return (y_prompt, y_sample, jnp.stack(kv_p), jnp.stack(kv_s), jnp.stack(win_p), jnp.stack(win_s),
            jnp.stack(ret_p), jnp.stack(ret_s))


_drawn_inputs = setup_inputs


def setup_inputs(seed=0):
    import zlib

    import numpy as np

    out = dict(_drawn_inputs(seed))
    spreads = {}
    factors = {'cmp_pos_k': 24.172, 'cmp_pos_v': 2.735, 'ln2': 4.082, 'ln_f': 8.03}
    for name, (base, spread) in spreads.items():
        noise = np.random.default_rng([zlib.crc32(name.encode()), seed]).standard_normal(out[name].shape)
        drawn = base * np.exp(spread * noise) if base else spread * noise
        out[name] = __import__('jax').numpy.asarray(drawn.astype(out[name].dtype))
    for name, factor in factors.items():
        out[name] = (out[name] * factor).astype(out[name].dtype)
    return out
```

```python
from contextlib import ExitStack

import concourse.bass as bass
import numpy as np
from concourse import mybir

F32 = mybir.dt.float32
I32 = mybir.dt.int32
ALU = mybir.AluOpType
ACT = mybir.ActivationFunctionType
AX = mybir.AxisListType

P = 128
DM = 1024
KT = DM // P
SEQ = 1024
NB_SEQ = 8
PAST = 2048
PAGE = 128
NPOOL = 160
HD = 64
NT = 9
TP = SEQ // P
TOK = SEQ + NB_SEQ
FF = 2816
NF = FF // P
TC = TOK // 3
WIN = 512
EPS = 1e-6
CH = 16
NEG = -1e30
NSEL = 33
NRANK = 30
TOP = 13

QW, KVW, GW, RW = 512, 768, 24, 512
KV0 = QW
R0 = QW + KVW + GW
CHUNKS = ["kv", "win", "q"] + [("ret", i) for i in range(4)]
NCH = len(CHUNKS)
WIDTH = [512, 256 + GW, 512] + [512] * 4
NI = NCH * NT
NRAW = 6
WORDS = 52900

CONST = {}


def constants():
    lg = np.log((1.0 - 2.0 ** (-5.0 - np.arange(8, dtype=np.float32))).astype(np.float32)).astype(np.float64)
    parts = []

    def put(name, a):
        a = np.asarray(a, np.float64).reshape(P, -1).astype(np.float32)
        CONST[name] = (sum(x.shape[1] for x in parts), a.shape[1])
        parts.append(a)

    p = np.arange(P)
    put("ident", np.eye(P))
    inv = (1.0 / (np.float32(10000.0) ** (np.arange(32, dtype=np.float32) / np.float32(32)))).astype(np.float32)
    pos = np.stack([i * P + p if i < TP else np.full(P, PAST) for i in range(NT)], 1).astype(np.float32)
    ang = (pos[:, :, None] * inv).astype(np.float32).astype(np.float64)
    put("rope", np.stack([np.cos(ang), -np.sin(ang), np.sin(ang)], 2))
    i = np.arange(P)
    diff = i[None, :] - p[:, None]
    put("dec", np.stack([np.where(diff >= 0, np.exp(np.maximum(diff, 0) * lg[h]), 0) * 0.125 for h in range(8)], 1))
    put("qdec", np.stack([np.stack([np.exp((i + 1) * lg[2 * hp + (d >= HD)]) for d in p]) for hp in range(4)], 1))
    put("kdec", np.stack([np.exp((P - 1 - p) * lg[h]) * 0.125 for h in range(8)], 1))
    put("gchunk", np.stack([np.exp(P * lg[2 * hp + (p >= HD)]) for hp in range(4)], 1))
    put("gone", np.exp(lg[p % 8]))
    put("causal", np.where(i[None, :] <= p[:, None], 0, NEG))
    put("edge", np.where(i[None, :] > p[:, None], 0, NEG))
    n = np.arange(63)
    put("cmp", np.stack([np.where(n[None, :] * CH + 31 <= t * P + p[:, None], 0, NEG) for t in range(TP)], 1))
    r = np.arange(NRANK)
    put("tie", np.broadcast_to((r[None, :] < r[:, None]).astype(float), (P, NRANK, NRANK)))
    put("group", np.where((p[:, None] // 4 == np.arange(8)[None, :] // 4), 1.0, 0.0))
    return np.ascontiguousarray(np.concatenate(parts, 1))


NCONST = constants().shape[1]



class Named:
    pass


class Semaphores:

    def __init__(self, nc, ctx):
        self.nc, self.ctx, self.by_name = nc, ctx, {}

    def __getitem__(self, name):
        if name not in self.by_name:
            self.by_name[name] = self.ctx.enter_context(self.nc.semaphore(name))
        return self.by_name[name]

    def wait(self, engine, name, value):
        if value > 0:
            engine.wait_ge(self[name], value)


class Links:

    def __init__(self, engine, s, name):
        self.engine, self.sem, self.count = engine, s[name], 0

    def after(self, instruction):
        self.count += 1
        instruction.then_inc(self.sem, 1)
        self.engine.wait_ge(self.sem, self.count)


class Room:

    def __init__(self, arena, start):
        self.arena, self.at = arena, start

    def __call__(self, n):
        v = self.arena[:, self.at:self.at + n]
        self.at += n
        assert self.at <= self.arena.shape[1], self.at
        return v


def rows(t):
    return P if t < TP else NB_SEQ


def place_memory(nc, ctx):
    arena = ctx.enter_context(nc.sbuf_tensor("arena", [P, WORDS], F32))
    m = Named()
    m.banks = ctx.enter_context(nc.psum_tensor("banks", [P, 8, 512], F32))
    room = Room(arena, 0)
    m.cst = room(NCONST)

    def const_of(name):
        at, n = CONST[name]
        return m.cst[:, at:at + n]

    m.ident = const_of("ident")
    m.rope = const_of("rope").rearrange("p (t s d) -> p t s d", t=NT, s=3)
    m.dec = const_of("dec").rearrange("p (h i) -> p h i", h=8)
    m.qdec = const_of("qdec").rearrange("p (h i) -> p h i", h=4)
    m.kdec, m.gchunk, m.gone = const_of("kdec"), const_of("gchunk"), const_of("gone")
    m.causal, m.edge = const_of("causal"), const_of("edge")
    m.cmp_mask = const_of("cmp").rearrange("p (t n) -> p t n", t=TP)
    m.tie = const_of("tie").rearrange("p (j i) -> p j i", j=NRANK)
    m.group = const_of("group")
    m.lnb = room(DM)
    m.small = room(256)
    after_const = room.at

    m.qT = room(4 * SEQ).rearrange("p (h t) -> p h t", h=4)
    m.qbd = room(64).rearrange("p (b r) -> p b r", b=8)
    m.kselT, m.kwinT = room(SEQ), room(SEQ)
    m.vsel = room(SEQ).rearrange("p (t n) -> p t n", t=TP)
    m.vwin = room(SEQ).rearrange("p (t n) -> p t n", t=TP)
    m.gates = room(NT * GW).rearrange("p (t n) -> p t n", t=NT)
    m.ksnew = room(8)
    m.gs = room(24).rearrange("p (b n) -> p b n", b=8)
    m.kcbP, m.vcbP = room(64), room(128)
    m.mixT = room(8 * TOK).rearrange("p (k t) -> p k t", k=8)
    after_mix = room.at

    a = Room(arena, after_mix)
    m.hT = a(8 * TOK).rearrange("p (k t) -> p k t", k=8)
    m.wch = [a(KT * 512).rearrange("p (k n) -> p k n", k=KT) for _ in range(2)]
    m.xt = [a(DM) for _ in range(2)]
    m.sq = a(DM)
    m.raw = [a(512) for _ in range(NRAW)]
    m.t1, m.t2 = [a(512) for _ in range(2)], [a(512) for _ in range(2)]
    m.qp = [a(512) for _ in range(2)]
    m.rT = [a(256).rearrange("p (a t) -> p a t", a=2) for _ in range(2)]
    m.qd = [a(128) for _ in range(2)]
    m.kd = [a(128) for _ in range(2)]
    m.att = [a(256).rearrange("p (a t) -> p a t", a=2) for _ in range(2)]
    m.state = [a(64) for _ in range(4)]
    m.oall = [m.mixT[:, 4 + i, 0:SEQ].rearrange("p (t n) -> p t n", t=TP) for i in range(4)]
    m.gall = [m.mixT[:, i, 0:SEQ].rearrange("p (t n) -> p t n", t=TP) for i in range(4)]

    r = Room(arena, after_mix)
    m.S0, m.S1, m.S2 = r(4096), r(4096), r(4096)
    m.R4 = r(256).rearrange("p (j e) -> p j e", j=4)
    m.rsm = r(512)
    m.rrow = r(512)
    m.rsq = r(4096)
    m.rst = r(128)

    b = Room(arena, after_mix)
    m.w1 = [b(4096).rearrange("p (k n) -> p k n", k=16) for _ in range(2)]
    m.cmpb = b(4096).rearrange("p (t n) -> p t n", t=CH)
    m.cmpg = b(4096).rearrange("p (v g t d) -> p v g t d", v=2, g=2, t=CH)
    m.selk, m.selv = (b(2048).rearrange("p (t n) -> p t n", t=CH) for _ in range(2))
    m.XT = b(2048).rearrange("p (j g c) -> p j g c", j=8, g=2)
    m.kselb = b(2048)
    m.wink, m.winv = (b(512).rearrange("p (t n) -> p t n", t=4) for _ in range(2))
    m.kwb = b(512)
    m.SR = b(2688)
    m.w2 = [b(128).rearrange("p (m n) -> p m n", m=2) for _ in range(2)]
    m.posT = [b(16) for _ in range(2)]
    m.cbias = b(4)
    m.pages = b(NB_SEQ * PAST // PAGE).bitcast(I32)
    m.G = [m.mixT[:, 0, 508 * i:508 * i + 508].rearrange("p (m n) -> p m n", m=2) for i in range(2)]
    m.cg = m.mixT[:, 1, 0:900].rearrange("p (j i) -> p j i", j=NRANK)
    m.ce = m.mixT[:, 2, 0:900].rearrange("p (j i) -> p j i", j=NRANK)
    x = Room(m.lnb, 0)
    m.kcb, m.vcb = [x(128), x(128)], [x(128), x(128)]
    m.PT = x(168)
    m.bst, m.imp, m.blkm, m.pcn = x(40), x(32), x(32), x(128)

    c = Room(arena, after_mix)
    m.wo = c(8 * DM).rearrange("p (k n) -> p k n", k=8)
    m.prob = [c(1024) for _ in range(3)]
    m.pts = [c(512) for _ in range(3)]
    m.oraw = c(24 * HD).rearrange("p (u d) -> p u d", u=24)
    m.osum = c(512)
    m.sums, m.rsc, m.nmax = [c(24), c(24)], c(24), c(8)

    d = Room(arena, c.at)
    m.h2T = d(8 * TOK).rearrange("p (k t) -> p k t", k=8)
    d2 = Room(arena, after_mix + 8 * DM)
    m.xr = [d2(DM) for _ in range(2)]
    m.dsq = d2(DM)
    m.dh = [d2(DM) for _ in range(2)]
    assert d2.at <= c.at

    e = Room(arena, after_const)
    m.aT = e(NF * TOK).rearrange("p (f t) -> p f t", f=NF)
    assert e.at <= c.at
    e = Room(arena, d.at)
    m.wgu = [e(2 * KT * P).rearrange("p (s k n) -> p s k n", s=2, k=KT) for _ in range(2)]
    m.sg = [e(TC) for _ in range(3)]
    e = Room(arena, d.at)
    m.wd = [e(NF * P).rearrange("p (f n) -> p f n", f=NF) for _ in range(2)]
    m.yT = m.h2T
    g = Room(arena, after_const)
    m.gx = [g(DM) for _ in range(3)]
    m.gsq = g(DM)
    return m


def is_ret(n):
    return 0 <= n < NI and isinstance(CHUNKS[n // NT], tuple) and n % NT < TP


def turns(n):
    if not 0 <= n < NI:
        return False
    kind = CHUNKS[n // NT]
    return kind in ("kv", "q") or (kind == "win" and n % NT < TP) or is_ret(n)


def turns_before(n):
    return sum(turns(k) for k in range(n))


def ret_before(n):
    return sum(is_ret(k) for k in range(n))


def stored(n):
    kind, t = CHUNKS[n // NT], n % NT
    if kind == "kv":
        return 1
    if kind == "win":
        return int(t >= TP - WIN // P)
    return 2 if isinstance(kind, tuple) and t == TP else 0


def stored_before(n):
    return sum(stored(k) for k in range(n % NRAW, n, NRAW))


def vkeep_before(n):
    return sum(1 for k in range(n) if CHUNKS[k // NT] in ("kv", "win") and k % NT < TP)


def heads(kind, ap):
    if kind == "kv":
        return ap[:, 0:512].rearrange("p (s v h d) -> p s v h d", s=2, v=2, h=2)[:, :, 0, :, :]
    n = 128 if kind == "win" else 512 if kind == "q" else 256
    return ap[:, 0:n].rearrange("p (s h d) -> p s h d", s=1, d=HD)


def stage_project(nc, s, m, io):
    wait = s.wait
    steps = range(NI + 3)
    with nc.Block() as block:

        @block.sync
        def _(sp):
            sp.dma_start(m.cst, io.const).then_inc(s["const_in"], 16)
            sp.dma_start(m.lnb, io.ln1[0:1, :].to_broadcast((P, DM))).then_inc(s["ln1_in"], 16)

            def load_chunk(ch):
                wait(sp, "proj_done", (ch - 1) * NT)
                kind, dst, done = CHUNKS[ch], m.wch[ch % 2], s[f"w_in{ch % 2}"]
                if isinstance(kind, tuple):
                    for j in range(4):
                        at = R0 + RW * j + P * kind[1]
                        sp.dma_start(dst[:, :, P * j:P * j + P], io.w_in[:, :, at:at + P]).then_inc(done, 16)
                else:
                    at = {"kv": KV0, "win": KV0 + 512, "q": 0}[kind]
                    sp.dma_start(dst[:, :, 0:WIDTH[ch]], io.w_in[:, :, at:at + WIDTH[ch]]).then_inc(done, 16)

            for i in range(NT):
                wait(sp, "turned", i - 1)
                src = io.xp[i * P:(i + 1) * P, :] if i < TP else io.xs
                sp.dma_start(m.xt[i % 2][0:rows(i), :], src).then_inc(s[f"x_in{i % 2}"], 16)
                if i == 1:
                    load_chunk(0)
                    load_chunk(1)
            for n in range(NI):
                kind, ch, t = CHUNKS[n // NT], n // NT, n % NT
                if t == 1 and 1 <= ch < NCH - 1:
                    load_chunk(ch + 1)
                if not stored(n):
                    continue
                slot, out = m.raw[n % NRAW], s[f"slot_out{n % NRAW}"]
                sp.wait_ge(s["roped"], n + 1)
                if kind == "kv":
                    dst = io.kvp[t * P:(t + 1) * P, :] if t < TP else io.kvs
                    sp.dma_start(dst, slot[0:rows(t), :]).then_inc(out, 16)
                elif kind == "win":
                    at = (t - TP + WIN // P) * P
                    dst = io.winp[at:at + P, :] if t < TP else io.wins[:, WIN - 1, :]
                    sp.dma_start(dst, slot[0:rows(t), 0:256]).then_inc(out, 16)
                else:
                    src = slot[0:NB_SEQ, :].rearrange("b (j h e) -> b h j e", j=4, h=2)
                    for h2 in range(2):
                        sp.dma_start(io.ret_rows[:, 2 * kind[1] + h2, :, :], src[:, h2, :, :]).then_inc(out, 16)
            sp.wait_ge(s["gate_done"], NT)
            sp.dma_start(io.gate_rows, m.gates[0:NB_SEQ, TP, :]).then_inc(s["gates_out"], 16)
            for hp in range(4):
                sp.wait_ge(s["state_done"], TP * (hp + 1))
                sp.dma_start(io.retp[hp], m.state[hp]).then_inc(s["state_out"], 16)
            sp.dma_start(io.wins[:, 0:WIN - 1, :], io.cwin[:, 1:WIN, :]).then_inc(s["wins_out"], 16)
            sp.wait_ge(s["gates_out"], 16)
            sp.wait_ge(s["state_out"], 64)
            sp.wait_ge(s["wins_out"], 16)
            for k in range(NRAW):
                wait(sp, f"slot_out{k}", 16 * stored_before(NI + (k - NI) % NRAW))

        @block.scalar
        def _(act):
            own = Links(act, s, "a_act")

            def norm(i):
                act.wait_ge(s[f"x_in{i % 2}"], 16 * (i // 2 + 1))
                r = rows(i)
                own.after(act.activation(m.sq[0:r, :], m.xt[i % 2][0:r, :], ACT.Square,
                                         accum_out=m.small[0:r, i:i + 1]))
                wait(act, "a_dve_const", 1)
                act.activation(m.small[0:r, 16 + i:17 + i], m.small[0:r, i:i + 1], ACT.Sqrt,
                               bias=m.small[0:r, 64:65], scale=1.0 / DM).then_inc(s["rms_done"], 1)

            norm(0)
            for n in range(NI):
                kind, t = CHUNKS[n // NT], n % NT
                r = rows(t)
                if n + 1 < NT:
                    norm(n + 1)
                if n < NT:
                    act.wait_ge(s["turned"], n + 1)
                    act.activation(m.hT[:, 4:8, n * P:n * P + r],
                                   m.banks[:, 2 + 2 * (n % 2), :].rearrange("p (k t) -> p k t", k=4)[:, :, 0:r],
                                   ACT.Copy).then_inc(s["hT_hi"], 1)
                slot, src = m.raw[n % NRAW], m.banks[:, 6 + n % 2, :]
                k = n - NRAW
                if k >= 0:
                    act.wait_ge(s["roped"], k + 1)
                    wait(act, "tturned", turns_before(k + 1))
                    wait(act, "vkept", vkeep_before(k + 1))
                    wait(act, "o_done", ret_before(k + 1))
                    wait(act, f"slot_out{n % NRAW}", 16 * stored_before(n))
                act.wait_ge(s["proj_done"], n + 1)
                if kind == "win":
                    act.activation(m.gates[0:r, t, :], src[0:r, 256:280], ACT.Sigmoid).then_inc(s["gate_done"], 1)
                    act.activation(slot[0:r, 0:256], src[0:r, 0:256], ACT.Copy).then_inc(s["raw_done"], 1)
                elif isinstance(kind, tuple):
                    dst = m.gall[kind[1]][:, t, :] if t < TP else slot[0:r, 384:512]
                    act.activation(dst, src[0:r, 384:512], ACT.Silu)
                    act.activation(slot[0:r, 0:384], src[0:r, 0:384], ACT.Copy).then_inc(s["raw_done"], 1)
                else:
                    act.activation(slot[0:r, :], src[0:r, :], ACT.Copy).then_inc(s["raw_done"], 1)

        @block.gpsimd
        def _(pool):
            pool.wait_ge(s["const_in"], 16)
            for n in steps:
                if n < NI:
                    kind, t = CHUNKS[n // NT], n % NT
                    r = rows(t)
                    slot = m.raw[n % NRAW][0:r, :]
                    x = heads(kind, slot).rearrange("p s h (w d) -> p s (h w) d", w=2)
                    y = heads(kind, m.t1[n % 2][0:r, :]).rearrange("p s h (w d) -> p s (h w) d", w=2)
                    cos = m.rope[0:r, t, 0:1, :].unsqueeze(1).broadcast_to(x.shape)
                    pool.wait_ge(s["raw_done"], n + 1)
                    wait(pool, "roped", n - 1)
                    pool.tensor_tensor(y, x, cos, ALU.mult).then_inc(s["cos_done"], 1)
                    if kind in ("kv", "win") and t < TP:
                        dst, at = (m.vsel, 384) if kind == "kv" else (m.vwin, 128)
                        pool.tensor_copy(dst[:, t, :], slot[:, at:at + 128]).then_inc(s["vkept"], 1)
                k = n - 2
                if is_ret(k):
                    hp = CHUNKS[k // NT][1]
                    pool.wait_ge(s["roped"], k + 1)
                    wait(pool, "o_done", ret_before(k) - 1)
                    pool.tensor_tensor(m.kd[ret_before(k) % 2].rearrange("p (h d) -> p h d", h=2),
                                       m.raw[k % NRAW][:, 128:256].rearrange("p (h d) -> p h d", h=2),
                                       m.kdec[:, 2 * hp:2 * hp + 2].unsqueeze(2).broadcast_to((P, 2, HD)),
                                       ALU.mult).then_inc(s["kd_done"], 1)

        @block.vector
        def _(dve):
            own = Links(dve, s, "a_dve")
            dve.memset(m.small[:, 64:65], EPS).then_inc(s["a_dve_const"], 1)
            own.after(dve.memset(m.qbd, 0.0))
            dve.wait_ge(s["ln1_in"], 16)

            def norm(i):
                r = rows(i)
                dve.wait_ge(s["rms_done"], i + 1)
                own.after(dve.reciprocal(m.small[0:r, 32 + i:33 + i], m.small[0:r, 16 + i:17 + i]))
                x = m.xt[i % 2][0:r, :]
                dve.scalar_tensor_tensor(out=x, in0=x, scalar=m.small[0:r, 32 + i:33 + i], in1=m.lnb[0:r, :],
                                         op0=ALU.mult, op1=ALU.mult).then_inc(s["h_done"], 1)

            norm(0)
            dve.wait_ge(s["const_in"], 16)
            for n in steps:
                if n < NI:
                    kind, t = CHUNKS[n // NT], n % NT
                    r = rows(t)
                    if n + 1 < NT:
                        norm(n + 1)
                    if n < NT:
                        dve.wait_ge(s["turned"], n + 1)
                        dve.tensor_copy(m.hT[:, 0:4, n * P:n * P + r],
                                        m.banks[:, 1 + 2 * (n % 2), :].rearrange("p (k t) -> p k t", k=4)[:, :, 0:r]
                                        ).then_inc(s["hT_lo"], 1)
                    slot = m.raw[n % NRAW][0:r, :]
                    x, y = heads(kind, slot), heads(kind, m.t2[n % 2][0:r, :])
                    c = heads(kind, m.t1[n % 2][0:r, :])
                    dve.wait_ge(s["raw_done"], n + 1)
                    wait(dve, "roped", n - 1)
                    shape = x[:, :, :, 0:32].shape
                    for half in range(2):
                        sin = m.rope[0:r, t, 1 + half:2 + half, :].unsqueeze(1).broadcast_to(shape)
                        own_in = dve.tensor_tensor(y[:, :, :, 32 * half:32 * half + 32],
                                                   x[:, :, :, 32 - 32 * half:64 - 32 * half], sin, ALU.mult)
                    own.after(own_in)
                    dve.wait_ge(s["cos_done"], n + 1)
                    if kind == "q":
                        wait(dve, "tturned", turns_before(n - 1))
                        out = m.qp[n % 2][0:r, :].rearrange("p (h g d) -> p g h d", h=4, g=2)
                        c, y = (v[:, 0, :, :].rearrange("p (g h) d -> p g h d", g=2) for v in (c, y))
                        dve.tensor_tensor(out, c, y, ALU.add).then_inc(s["roped"], 1)
                    else:
                        dve.tensor_tensor(x, c, y, ALU.add).then_inc(s["roped"], 1)
                k = n - 1
                if turns(k):
                    kind, t = CHUNKS[k // NT], k % NT
                    dve.wait_ge(s["tturned"], turns_before(k) + 1)
                    src = m.banks[:, 0, :]
                    if kind == "kv" and t < TP:
                        last = dve.tensor_copy(m.kselT[:, t * P:(t + 1) * P], src[:, 0:P])
                    elif kind == "kv":
                        last = dve.tensor_copy(m.ksnew, src[:, 0:NB_SEQ])
                    elif kind == "win":
                        last = dve.tensor_copy(m.kwinT[:, t * P:(t + 1) * P], src[:, 0:P])
                    elif kind == "q" and t < TP:
                        last = dve.tensor_scalar(m.qT[:, :, t * P:(t + 1) * P], src.rearrange("p (h t) -> p h t", h=4),
                                                 0.125, None, ALU.mult)
                    elif kind == "q":
                        for g in range(2):
                            last = dve.tensor_scalar(
                                m.qbd[64 * g:64 * g + 64, :, 4 * g:4 * g + 4],
                                src[64 * g:64 * g + 64, :].rearrange("p (h t) -> p t h", h=4)[:, 0:NB_SEQ, :],
                                0.125, None, ALU.mult)
                    else:
                        j = ret_before(k) % 2
                        wait(dve, "o_done", ret_before(k) - 1)
                        dve.tensor_copy(m.rT[j], src[:, 0:256].rearrange("p (a t) -> p a t", a=2))
                        last = dve.tensor_tensor(m.qd[j], src[:, 0:P], m.qdec[:, kind[1], :], ALU.mult)
                    last.then_inc(s["tkept"], 1)
                k = n - 2
                if is_ret(k):
                    hp, j = CHUNKS[k // NT][1], ret_before(k)
                    dve.wait_ge(s["att_done"], j + 1)
                    wait(dve, "o_done", j - 1)
                    dve.tensor_tensor(m.att[j % 2], m.banks[:, 1:3, 0:P], m.dec[:, 2 * hp:2 * hp + 2, :],
                                      ALU.mult).then_inc(s["att_masked"], 1)
                k = n - 3
                if is_ret(k):
                    hp, t, j = CHUNKS[k // NT][1], k % NT, ret_before(k)
                    dve.wait_ge(s["o_done"], j + 1)
                    dve.tensor_copy(m.oall[hp][:, t, :].rearrange("p (h d) -> p h d", h=2), m.banks[:, 3:5, 0:HD])
                    for h2 in range(2):
                        at = slice(64 * h2, 64 * h2 + 64)
                        new = m.banks[at, 5, 64 * h2:64 * h2 + 64]
                        if t == 0:
                            last = dve.tensor_copy(m.state[hp][at, :], new)
                        else:
                            last = dve.scalar_tensor_tensor(out=m.state[hp][at, :], in0=m.state[hp][at, :],
                                                            scalar=m.gchunk[at, hp:hp + 1], in1=new,
                                                            op0=ALU.mult, op1=ALU.add)
                    last.then_inc(s["state_done"], 1)

        @block.tensor
        def _(pe):
            pe.wait_ge(s["const_in"], 16)
            for n in steps:
                if n < NI:
                    kind, ch, t = CHUNKS[n // NT], n // NT, n % NT
                    r = rows(t)
                    if n < NT:
                        pe.wait_ge(s["h_done"], n + 1)
                        wait(pe, "hT_lo", n - 1)
                        wait(pe, "hT_hi", n - 1)
                        for k in range(KT):
                            b = 1 + 2 * (n % 2) + k // 4
                            last = pe.transpose(m.banks[:, b, P * (k % 4):P * (k % 4) + r],
                                                m.xt[n % 2][0:r, k * P:(k + 1) * P], m.ident[0:r, 0:r])
                        last.then_inc(s["turned"], 1)
                    if t == 0:
                        per = [1, 1, 1, 4, 4, 4, 4]
                        pe.wait_ge(s[f"w_in{ch % 2}"], 16 * sum(per[ch % 2:ch + 1:2]))
                    if n < NT:
                        pe.wait_ge(s["hT_lo"], n + 1)
                        pe.wait_ge(s["hT_hi"], n + 1)
                    wait(pe, "raw_done", n - 1)
                    for k in range(KT):
                        last = pe.matmul(m.banks[0:r, 6 + n % 2, 0:WIDTH[ch]], m.hT[:, k, t * P:t * P + r],
                                         m.wch[ch % 2][:, k, 0:WIDTH[ch]], start=(k == 0), stop=(k == KT - 1))
                    last.then_inc(s["proj_done"], 1)
                k = n - 1
                if turns(k):
                    kind, t = CHUNKS[k // NT], k % NT
                    r = rows(t)
                    pe.wait_ge(s["roped"], k + 1)
                    wait(pe, "tkept", turns_before(k))
                    if kind == "q":
                        src, cols = m.qp[k % 2], [0, 128, 256, 384]
                    else:
                        src, cols = m.raw[k % NRAW], [256] if kind == "kv" else [0] if kind == "win" else [0, 128]
                    for i, at in enumerate(cols):
                        last = pe.transpose(m.banks[:, 0, P * i:P * i + r], src[0:r, at:at + P], m.ident[0:r, 0:r])
                    last.then_inc(s["tturned"], 1)
                k = n - 2
                if is_ret(k):
                    j = ret_before(k)
                    pe.wait_ge(s["tkept"], turns_before(k) + 1)
                    wait(pe, "att_masked", j)
                    for h2 in range(2):
                        at = slice(64 * h2, 64 * h2 + 64)
                        last = pe.matmul(m.banks[:, 1 + h2, 0:P], m.rT[j % 2][at, 1, :], m.rT[j % 2][at, 0, :],
                                         start=True, stop=True)
                    last.then_inc(s["att_done"], 1)
                k = n - 3
                if is_ret(k):
                    hp, t, j = CHUNKS[k // NT][1], k % NT, ret_before(k)
                    v = m.raw[k % NRAW][:, 256:384]
                    pe.wait_ge(s["att_masked"], j + 1)
                    pe.wait_ge(s["kd_done"], j + 1)
                    wait(pe, "state_done", j)
                    for h2 in range(2):
                        at = slice(64 * h2, 64 * h2 + 64)
                        o = m.banks[:, 3 + h2, 0:HD]
                        pe.matmul(o, m.att[j % 2][:, h2, :], v[:, at], start=True, stop=(t == 0))
                        if t > 0:
                            pe.matmul(o, m.qd[j % 2][at, :], m.state[hp][at, :], start=False, stop=True)
                    pe.matmul(m.banks[:, 5, 0:P], m.kd[j % 2], v, start=True, stop=True).then_inc(s["o_done"], 1)


STEPS_B = range(NB_SEQ + 3)
SEQS_B = range(NB_SEQ + 1)


def chunks_of(q):
    return (SEQ if q == 0 else PAST) // CH


def turn_uses():
    uses = []
    for step in STEPS_B:
        a = step - 1
        if step in SEQS_B:
            uses += [("k", step, i) for i in range(4)]
        if 1 <= a <= NB_SEQ:
            uses += [("s", a, i) for i in range(5)]
        if step in SEQS_B:
            uses += [("v", step, i) for i in range(4)]
    return uses


TURNS = turn_uses()
TURN_AT = {u: i for i, u in enumerate(TURNS)}


def kept_by(count, dve):
    return sum((u[0] == "s") == dve for u in TURNS[:count])


def stage_sequences(nc, s, m, io):
    wait = s.wait
    NPG = PAST // PAGE
    CMP, SEL, WINC = slice(0, 127), slice(127, 2176), slice(2176, 2688)
    SR = m.SR[0:8, :]
    bst = m.bst[0:8, :]

    def free_turn_bank(eng, i):
        if i >= 2:
            wait(eng, "b_kept_dve", kept_by(i - 1, True))
            wait(eng, "b_kept_act", kept_by(i - 1, False))

    with nc.Block() as block:

        @block.sync
        def _(sp):
            for kv in range(2):
                sp.dma_start(m.w1[kv], io.w1[kv]).then_inc(s["b_weights_in"], 16)
                sp.dma_start(m.w2[kv], io.w2[kv]).then_inc(s["b_weights_in"], 16)
                with nc.allow_non_contiguous_dma(reason="the 32 x 64 position rows, turned"):
                    sp.dma_start(m.posT[kv], io.pos[kv]).then_inc(s["b_weights_in"], 16)
            sp.dma_start(m.cmpb[0:64, :, :], io.kvp.rearrange("(c t) n -> c t n", t=CH)[:, :, 0:256]
                         ).then_inc(s["cmp_in"], 16)
            sp.dma_start(m.pages[0:1, :], io.table).then_inc(s["pages_in"], 16)
            sp.wait_ge(s["pages_in"], 16)

            def pages(q, dst, lo, n, done):
                for pg in range(NPG):
                    at = NPG * (q - 1) + pg
                    page = sp.value_load(m.pages[0:1, at:at + 1], min_val=0, max_val=NPOOL - 1)
                    sp.dma_start(dst[8 * pg:8 * pg + 8, :, :],
                                 io.pool[bass.ds(page, 1), :, :, lo:lo + n].rearrange("a c t n -> (a c) t n")
                                 ).then_inc(s[done], 16)

            for step in STEPS_B:
                q = step + 1
                if q <= NB_SEQ:
                    sp.wait_ge(s["b_grouped"], 2 * q)
                    pages(q, m.cmpb, 0, 256, "cmp_in")
                q = step - 1
                if 1 <= q <= NB_SEQ:
                    wait(sp, "pv_done", q - 1)
                    pages(q, m.selv, 384, 128, "selv_in")
                    sp.dma_start(m.winv, io.wins[q - 1, :, :].rearrange("(p t) n -> p t n", t=4)[:, :, 128:256]
                                 ).then_inc(s["winv_in"], 16)
                    sp.dma_start(m.vcb[q % 2][127:128, :], io.kvs[q - 1:q, 384:512]).then_inc(s["vnew_in"], 16)

        @block.gpsimd
        def _(pool):
            pool.wait_ge(s["pages_in"], 16)
            for q in SEQS_B:
                for kv in range(2):
                    n = chunks_of(q)
                    pool.wait_ge(s["cmp_in"], 16 + 16 * NPG * q)
                    if q:
                        pool.wait_ge(s["b_turned"], TURN_AT["kv"[kv], q - 1, 3] + 1)
                    pool.tensor_copy(m.cmpg[0:n, kv, :, :, :],
                                     m.cmpb[0:n, :, P * kv:P * kv + P].rearrange("p t (g d) -> p g t d", g=2)
                                     ).then_inc(s["b_grouped"], 1)
                if q == 0:
                    continue
                if q >= 2:
                    pool.wait_ge(s["b_turned"], TURN_AT["s", q - 1, 4] + 1)
                for pg in range(NPG):
                    at = NPG * (q - 1) + pg
                    page = pool.value_load(m.pages[0:1, at:at + 1], min_val=0, max_val=NPOOL - 1)
                    pool.dma_start(m.selk[8 * pg:8 * pg + 8, :, :],
                                   io.pool[bass.ds(page, 1), :, :, 256:384].rearrange("a c t n -> (a c) t n")
                                   ).then_inc(s["selk_in"], 16)
                pool.dma_start(m.wink, io.wins[q - 1, :, :].rearrange("(p t) n -> p t n", t=4)[:, :, 0:128]
                               ).then_inc(s["wink_in"], 16)

        @block.tensor
        def _(pe):
            pe.wait_ge(s["b_weights_in"], 96)
            for kv in range(2):
                for mt in range(2):
                    for k in range(16):
                        last = pe.matmul(m.banks[:, 2 + mt, kv:kv + 1], m.w1[kv][:, k, P * mt:P * mt + P],
                                         m.posT[kv][:, k:k + 1], start=(k == 0), stop=(k == 15))
            last.then_inc(s["b_bias"], 1)

            def compress(q, kv):
                nch = chunks_of(q)
                nb = nch - 1
                pe.wait_ge(s["b_grouped"], 2 * q + kv + 1)
                for i in range(4):
                    u = TURN_AT["kv"[kv], q, i]
                    free_turn_bank(pe, u)
                    for x in range(4):
                        t = 4 * i + 2 * (x // 2)
                        src = m.cmpg[0:nch, kv, x % 2, t:t + 2, :].rearrange("p t d -> p (t d)")
                        last = pe.transpose(m.banks[:, u % 2, P * x:P * x + nch], src, m.ident[0:nch, 0:nch])
                    last.then_inc(s["b_turned"], 1)
                done = 2 * q + kv
                pe.wait_ge(s["b_gelu"], 2 * done) if done else pe.wait_ge(s["b_bias_kept"], 1)
                for i in range(4):
                    pe.wait_ge(s["b_kept_act"], kept_by(TURN_AT["kv"[kv], q, i] + 1, False))
                    for k in (2 * i, 2 * i + 1, 8 + 2 * i, 9 + 2 * i):
                        for mt in range(2):
                            last = pe.matmul(m.banks[:, 2 + mt, 0:2 * nb], m.w1[kv][:, k, P * mt:P * mt + P],
                                             m.XT[:, k % 8, :, k // 8:k // 8 + nb], start=(k == 0), stop=(k == 15))
                last.then_inc(s["b_hidden"], 1)

            def compressed(q):
                nb = chunks_of(q) - 1
                pe.wait_ge(s["b_gelu"], 4 * q + 4)
                wait(pe, "pv_kept", q - 2)
                wait(pe, "pt_kept", q - 2)
                for g in range(2):
                    for mt in range(2):
                        last = pe.matmul(m.banks[64 * g:64 * g + 64, 4, 0:nb], m.w2[0][:, mt, :],
                                         m.G[0][:, mt, nb * g:nb * g + nb], start=(mt == 0), stop=(mt == 1))
                last.then_inc(s["b_kc"], 1)
                for g in range(2):
                    for mt in range(2):
                        last = pe.matmul(m.banks[0:nb, 5, 64 * g:64 * g + 64], m.G[1][:, mt, nb * g:nb * g + nb],
                                         m.w2[1][:, mt, :], start=(mt == 0), stop=(mt == 1))
                last.then_inc(s["b_vc"], 1)

            def values(q):
                pe.wait_ge(s["b_scaled"], q)
                wait(pe, "b_vc_kept", q + 2 if q + 1 <= NB_SEQ else q + 1)
                for i in range(21):
                    last = pe.transpose(m.banks[:, 5, 8 * i:8 * i + 8], SR[:, P * i:P * i + P], m.ident[0:8, 0:8])
                last.then_inc(s["pt_done"], 1)
                pe.wait_ge(s["pt_kept"], q)
                pe.wait_ge(s["selv_in"], 16 * NPG * q)
                pe.wait_ge(s["winv_in"], 16 * q)
                pe.wait_ge(s["vnew_in"], 16 * q)
                for i in range(21):
                    v = m.vcb[q % 2] if i == 0 else m.selv[:, i - 1, :] if i <= CH else m.winv[:, i - 1 - CH, :]
                    last = pe.matmul(m.banks[:, 4, 0:8], v, m.PT[:, 8 * i:8 * i + 8], start=(i == 0), stop=(i == 20))
                last.then_inc(s["pv_done"], 1)

            def scores(q):
                pe.wait_ge(s["selk_in"], 16 * NPG * q)
                pe.wait_ge(s["wink_in"], 16 * q)
                for i in range(5):
                    u = TURN_AT["s", q, i]
                    free_turn_bank(pe, u)
                    for x in range(4):
                        src = m.selk[:, 4 * i + x, :] if i < 4 else m.wink[:, x, :]
                        last = pe.transpose(m.banks[:, u % 2, P * x:P * x + P], src, m.ident)
                    last.then_inc(s["b_turned"], 1)
                pe.wait_ge(s["b_kc_kept"], q + 1)
                wait(pe, "b_imp_read", q - 1)
                for i in range(6):
                    if i >= 1:
                        pe.wait_ge(s["b_kept_dve"], kept_by(TURN_AT["s", q, i - 1] + 1, True))
                    wait(pe, "sc_kept", 6 * (q - 1) + i - 1)
                    rhs = m.kcb[q % 2] if i == 0 else m.kselb[:, 512 * i - 512:512 * i] if i < 5 else m.kwb
                    n = 128 if i == 0 else 512
                    pe.matmul(m.banks[0:8, 6 + i % 2, 0:n], m.qbd[:, q - 1, :], rhs, start=True, stop=True
                              ).then_inc(s["sc_done"], 1)

            def importance(q):
                pe.wait_ge(s["b_pc"], q)
                pe.wait_ge(s["sc_kept"], 6 * q)
                pe.matmul(m.banks[0:8, 6, 0:127], m.group[0:8, :], m.pcn[0:8, 0:127], start=True, stop=True
                          ).then_inc(s["b_imp"], 1)

            for step in STEPS_B:
                if step in SEQS_B:
                    compress(step, 0)
                if 1 <= step - 2 <= NB_SEQ:
                    values(step - 2)
                if 1 <= step - 1 <= NB_SEQ:
                    scores(step - 1)
                if step in SEQS_B:
                    compress(step, 1)
                if 1 <= step - 1 <= NB_SEQ:
                    importance(step - 1)
                if step in SEQS_B:
                    compressed(step)

        @block.scalar
        def _(act):
            act.wait_ge(s["b_bias"], 1)
            act.activation(m.cbias.rearrange("p (m k) -> p m k", m=2), m.banks[:, 2:4, 0:2], ACT.Copy
                           ).then_inc(s["b_bias_kept"], 1)
            act.wait_ge(s["b_bias_kept"], 1)

            def keep_turned(q, kv):
                nch = chunks_of(q)
                if 2 * q + kv:
                    act.wait_ge(s["b_hidden"], 2 * q + kv)
                for i in range(4):
                    u = TURN_AT["kv"[kv], q, i]
                    act.wait_ge(s["b_turned"], u + 1)
                    act.activation(m.XT[:, 2 * i:2 * i + 2, :, 0:nch],
                                   m.banks[:, u % 2, :].rearrange("p (j g c) -> p j g c", j=2, g=2)[:, :, :, 0:nch],
                                   ACT.Copy).then_inc(s["b_kept_act"], 1)

            def gelu(q, kv):
                nb = chunks_of(q) - 1
                act.wait_ge(s["b_hidden"], 2 * q + kv + 1)
                wait(act, "b_vc", q)
                for mt in range(2):
                    act.activation(m.G[kv][:, mt, 0:2 * nb], m.banks[:, 2 + mt, 0:2 * nb], ACT.Gelu_apprx_tanh,
                                   bias=m.cbias[:, 2 * mt + kv:2 * mt + kv + 1]).then_inc(s["b_gelu"], 1)

            for step in STEPS_B:
                q = step - 2
                if step in SEQS_B:
                    keep_turned(step, 0)
                if 1 <= q <= NB_SEQ:
                    act.wait_ge(s["b_win_max"], q)
                    act.activation(SR[:, WINC], SR[:, WINC], ACT.Exp, bias=bst[:, 3:4],
                                   accum_out=bst[:, 4:5]).then_inc(s["b_win_exp"], 1)
                    act.wait_ge(s["b_sel_max"], q)
                    act.activation(SR[:, SEL], SR[:, SEL], ACT.Exp, bias=bst[:, 5:6],
                                   accum_out=bst[:, 6:7]).then_inc(s["b_sel_exp"], 1)
                if step in SEQS_B:
                    gelu(step, 0)
                q = step - 1
                if 1 <= q <= NB_SEQ:
                    wait(act, "pt_done", q - 1)
                    for i in range(6):
                        act.wait_ge(s["sc_done"], 6 * (q - 1) + i + 1)
                        at, n = (0, 128) if i == 0 else (128 + 512 * (i - 1), 512)
                        act.activation(SR[:, at:at + n], m.banks[0:8, 6 + i % 2, 0:n], ACT.Copy
                                       ).then_inc(s["sc_kept"], 1)
                    act.wait_ge(s["b_cmp_max"], q)
                    act.activation(SR[:, CMP], SR[:, CMP], ACT.Exp, bias=bst[:, 0:1],
                                   accum_out=bst[:, 1:2]).then_inc(s["b_cmp_exp"], 1)
                q = step
                if q in SEQS_B:
                    nb = chunks_of(q) - 1
                    keep_turned(q, 1)
                    gelu(q, 1)
                    kc, vc = (m.kcbP, m.vcbP) if q == 0 else (m.kcb[q % 2], m.vcb[q % 2])
                    act.wait_ge(s["b_kc"], q + 1)
                    if q:
                        act.activation(kc[:, 127:128], m.ksnew[:, q - 1:q], ACT.Copy)
                    act.activation(kc[:, 0:nb], m.banks[:, 4, 0:nb], ACT.Copy).then_inc(s["b_kc_kept"], 1)
                    act.wait_ge(s["b_vc"], q + 1)
                    wait(act, "pv_done", q - 2)
                    act.activation(vc[0:nb, :], m.banks[0:nb, 5, 0:128], ACT.Copy).then_inc(s["b_vc_kept"], 1)

        @block.vector
        def _(dve):
            own = Links(dve, s, "b_dve")
            own.after(dve.memset(m.blkm[0:8, :], 0.0))

            def inverse(total, gate, out):
                own.after(dve.tensor_scalar(total, total, 1e-30, None, ALU.max))
                own.after(dve.reciprocal(total, total))
                if gate is not None:
                    own.after(dve.tensor_tensor(out, total, gate, ALU.mult))

            for step in STEPS_B:
                q = step - 2
                if 1 <= q <= NB_SEQ:
                    dve.wait_ge(s["b_win_exp"], q)
                    inverse(bst[:, 4:5], m.gs[0:8, q - 1, 2:3], bst[:, 7:8])
                    dve.tensor_scalar(SR[:, WINC], SR[:, WINC], bst[:, 7:8], None, ALU.mult)
                    dve.wait_ge(s["b_sel_exp"], q)
                    inverse(bst[:, 6:7], m.gs[0:8, q - 1, 1:2], bst[:, 8:9])
                    dve.tensor_scalar(SR[:, SEL], SR[:, SEL], bst[:, 8:9], None, ALU.mult).then_inc(s["b_scaled"], 1)
                    dve.wait_ge(s["pt_done"], q)
                    wait(dve, "pv_done", q - 1)
                    dve.tensor_copy(m.PT, m.banks[:, 5, 0:168]).then_inc(s["pt_kept"], 1)
                    dve.wait_ge(s["pv_done"], q)
                    for g in range(2):
                        at = slice(64 * g, 64 * g + 64)
                        last = dve.tensor_copy(m.mixT[at, 0:4, SEQ + q - 1:SEQ + q].rearrange("p h t -> p (h t)"),
                                               m.banks[at, 4, 4 * g:4 * g + 4])
                    last.then_inc(s["pv_kept"], 1)
                q = step - 1
                if 1 <= q <= NB_SEQ:
                    wait(dve, "sc_done", 6 * (q - 1))
                    for i in range(5):
                        u = TURN_AT["s", q, i]
                        dve.wait_ge(s["b_turned"], u + 1)
                        dst = m.kselb[:, 512 * i:512 * i + 512] if i < 4 else m.kwb
                        dve.tensor_copy(dst, m.banks[:, u % 2, :]).then_inc(s["b_kept_dve"], 1)
                    dve.wait_ge(s["sc_kept"], 6 * (q - 1) + 1)
                    dve.tensor_reduce(bst[:, 0:1], SR[:, CMP], AX.X, ALU.max, negate=True).then_inc(s["b_cmp_max"], 1)
                    dve.wait_ge(s["sc_kept"], 6 * q)
                    dve.tensor_reduce(bst[:, 3:4], SR[:, WINC], AX.X, ALU.max, negate=True).then_inc(s["b_win_max"], 1)
                    dve.wait_ge(s["b_cmp_exp"], q)
                    inverse(bst[:, 1:2], None, None)
                    dve.tensor_scalar(m.pcn[0:8, 0:127], SR[:, CMP], bst[:, 1:2], None, ALU.mult).then_inc(s["b_pc"], 1)
                    dve.wait_ge(s["b_pc"], q)
                    own.after(dve.tensor_scalar(SR[:, CMP], m.pcn[0:8, 0:127], m.gs[0:8, q - 1, 0:1], None, ALU.mult))
                    dve.wait_ge(s["b_imp"], q)
                    imp, by = m.imp[0:8, 0:NRANK], m.banks[0:8, 6, :]
                    own.after(dve.tensor_reduce(imp, by[:, 4:124].rearrange("p (j n) -> p j n", n=4), AX.X, ALU.add))
                    dve.tensor_tensor(imp, by[:, 0:120].rearrange("p (j n) -> p j n", n=4)[:, :, 3], imp, ALU.add
                                      ).then_inc(s["b_imp_read"], 1)
                    dve.wait_ge(s["b_imp_read"], q)
                    other = imp.unsqueeze(1).broadcast_to((8, NRANK, NRANK))
                    mine = imp.unsqueeze(2).broadcast_to((8, NRANK, NRANK))
                    cg, ce = m.cg[0:8], m.ce[0:8]
                    dve.tensor_tensor(cg, other, mine, ALU.is_gt)
                    own.after(dve.tensor_tensor(ce, other, mine, ALU.is_equal))
                    own.after(dve.tensor_tensor(ce, ce, m.tie[0:8], ALU.mult))
                    own.after(dve.tensor_tensor(cg, cg, ce, ALU.add))
                    own.after(dve.tensor_reduce(imp, cg, AX.X, ALU.add))
                    own.after(dve.tensor_scalar(m.blkm[0:8, 1:1 + NRANK], imp, TOP - 0.5, NEG, ALU.is_gt, ALU.mult))
                    keys = SR[:, 128:2176].rearrange("p (t b c) -> p t b c", t=CH, c=4)
                    own.after(dve.tensor_tensor(keys, keys,
                                                m.blkm[0:8, :].unsqueeze(1).unsqueeze(3).broadcast_to(keys.shape), ALU.add))
                    dve.tensor_reduce(bst[:, 5:6], SR[:, SEL], AX.X, ALU.max, negate=True).then_inc(s["b_sel_max"], 1)


UNITS = [(t, hh, g, br) for t in range(TP) for hh in range(4) for g in range(2) for br in range(3)]
PER_TILE = 24


def key_tiles(u):
    t, _, _, br = UNITS[u]
    return 1 if br == 0 else t + 1 if br == 1 else min(t, 4) + 1


def attention_events():
    turn, events = [], [("S", 0)]

    def add(what):
        turn.append(what)
        events.append(("T", len(turn) - 1))
        if len(turn) > 1 and turn[-2][0] != "mix":
            events.append(("V", len(turn) - 2))
            u, first, n = turn[-2]
            if u % PER_TILE == PER_TILE - 1 and first + n == key_tiles(u):
                events.append(("E", UNITS[u][0]))

    for u in range(len(UNITS)):
        if u + 1 < len(UNITS):
            events.append(("S", u + 1))
        for first in range(0, key_tiles(u), 4):
            add((u, first, min(4, key_tiles(u) - first)))
        if u % PER_TILE == 5 and u > PER_TILE:
            add(("mix", UNITS[u][0] - 1))
    events += [("V", len(turn) - 1), ("E", TP - 1)]
    turn.append(("mix", TP - 1))
    events.append(("T", len(turn) - 1))
    return turn, events


TURNS_C, EVENTS_C = attention_events()


def on_dve(i):
    return TURNS_C[i][0] != "mix" and i % 2 == 0


def copied_before(i, dve):
    return sum(on_dve(k) == dve for k in range(i))


def values_before(i):
    return sum(TURNS_C[k][0] != "mix" for k in range(i))


def stage_attention(nc, s, m, io):
    wait = s.wait

    def scores_of(u, n):
        b = 2 * (u % 2)
        return m.banks[:, b:b + 2, :].rearrange("p a n -> p (a n)")[:, 0:n]

    def width(u):
        return 63 if UNITS[u][3] == 0 else P * key_tiles(u)

    def ends_block(i):
        u, first, n = TURNS_C[i]
        return u % 8 == 7 and first + n == key_tiles(u)

    with nc.Block() as block:

        @block.sync
        def _(sp):
            for g in range(2):
                sp.dma_start(m.wo[64 * g:64 * g + 64, 0:4, :],
                             io.w_out[256 * g:256 * g + 256, :].rearrange("(h d) n -> d h n", d=HD)).then_inc(s["wo_in"], 16)
            sp.dma_start(m.wo[:, 4:8, :], io.w_out[512:1024, :].rearrange("(h p) n -> p h n", p=P)).then_inc(s["wo_in"], 16)
            sp.dma_start(m.lnb, io.ln2[0:1, :].to_broadcast((P, DM))).then_inc(s["ln2_in"], 16)

        @block.tensor
        def _(pe):
            for what, i in EVENTS_C:
                if what == "S":
                    t, hh, g, br = UNITS[i]
                    at, q = slice(64 * g, 64 * g + 64), slice(P * t, P * t + P)
                    wait(pe, "c_exp", i - 1)
                    first = P * (t + 1) - width(i)
                    keys = m.kcbP if br == 0 else m.kselT if br == 1 else m.kwinT[:, first:first + width(i)]
                    out = scores_of(i, width(i))
                    for lo in range(0, width(i), 512):
                        hi = min(lo + 512, width(i))
                        last = pe.matmul(out[:, lo:hi], m.qT[at, hh, q], keys[at, lo:hi], start=True, stop=True)
                    last.then_inc(s["c_scores"], 1)
                elif what == "T":
                    wait(pe, "c_kept_dve", copied_before(i - 1, True))
                    wait(pe, "c_kept_act", copied_before(i - 1, False))
                    if TURNS_C[i][0] == "mix":
                        pe.wait_ge(s["c_osum"], TURNS_C[i][1] + 1)
                        for x in range(4):
                            last = pe.transpose(m.banks[:, 4 + i % 2, P * x:P * x + P], m.osum[:, P * x:P * x + P], m.ident)
                    else:
                        u, first, n = TURNS_C[i]
                        w = min(P, width(u))
                        pe.wait_ge(s["c_exp"], u + 1)
                        for x in range(n):
                            last = pe.transpose(m.banks[0:w, 4 + i % 2, P * x:P * x + P],
                                                m.prob[u % 3][:, P * (first + x):P * (first + x) + w], m.ident)
                    last.then_inc(s["c_turned"], 1)
                elif what == "V":
                    u, first, n = TURNS_C[i]
                    t, hh, g, br = UNITS[u]
                    w = min(P, width(u))
                    wait(pe, "c_okept", u // 8 - 1)
                    wait(pe, "c_kept_dve" if on_dve(i) else "c_kept_act", copied_before(i + 1, on_dve(i)))
                    for x in range(n):
                        k = first + x + (t + 1 - key_tiles(u) if br == 2 else 0)
                        v = m.vcbP if br == 0 else m.vsel[:, k, :] if br == 1 else m.vwin[:, k, :]
                        last = pe.matmul(m.banks[:, 6 + u // 8 % 2, 64 * (u % 8):64 * (u % 8) + 64],
                                         m.pts[i % 3][0:w, P * x:P * x + P], v[0:w, 64 * g:64 * g + 64],
                                         start=(first + x == 0), stop=(first + x == key_tiles(u) - 1))
                    last.then_inc(s["c_pv"], 1)

        @block.scalar
        def _(act):
            for what, i in EVENTS_C:
                if what == "S":
                    act.wait_ge(s["c_max"], i + 1)
                    if i >= 3:
                        act.wait_ge(s["c_turned"], 1 + max(k for k, x in enumerate(TURNS_C) if x[0] == i - 3))
                    wait(act, "c_inverted", UNITS[i][0] - 1)
                    act.activation(m.prob[i % 3][:, 0:width(i)], scores_of(i, width(i)), ACT.Exp,
                                   bias=m.nmax[:, i % 8:i % 8 + 1],
                                   accum_out=m.sums[UNITS[i][0] % 2][:, i % PER_TILE:i % PER_TILE + 1]
                                   ).then_inc(s["c_exp"], 1)
                elif what == "T" and not on_dve(i):
                    act.wait_ge(s["c_turned"], i + 1)
                    if TURNS_C[i][0] == "mix":
                        t = TURNS_C[i][1]
                        act.activation(m.mixT[:, 0:4, P * t:P * t + P],
                                       m.banks[:, 4 + i % 2, :].rearrange("p (h t) -> p h t", h=4), ACT.Copy
                                       ).then_inc(s["c_kept_act"], 1)
                    else:
                        u, first, n = TURNS_C[i]
                        w = min(P, width(u))
                        wait(act, "c_pv", values_before(i - 2))
                        act.activation(m.pts[i % 3][0:w, 0:P * n], m.banks[0:w, 4 + i % 2, 0:P * n], ACT.Copy
                                       ).then_inc(s["c_kept_act"], 1)
                elif what == "V" and ends_block(i):
                    b = TURNS_C[i][0] // 8
                    act.wait_ge(s["c_pv"], values_before(i + 1))
                    wait(act, "c_osum", b // 3)
                    act.activation(m.oraw[:, 8 * (b % 3):8 * (b % 3) + 8, :],
                                   m.banks[:, 6 + b % 2, :].rearrange("p (u d) -> p u d", u=8), ACT.Copy
                                   ).then_inc(s["c_okept"], 1)

        @block.gpsimd
        def _(pool):
            for t in range(TP):
                pool.wait_ge(s["c_inverted"], t + 1)
                pool.wait_ge(s["c_okept"], 3 * t + 3)
                pool.tensor_tensor(m.oraw, m.oraw, m.rsc.unsqueeze(2).broadcast_to((P, PER_TILE, HD)), ALU.mult
                                   ).then_inc(s["c_weighted"], 1)

        @block.vector
        def _(dve):
            own = Links(dve, s, "c_dve")
            for what, i in EVENTS_C:
                if what == "S":
                    t, hh, g, br = UNITS[i]
                    n = width(i)
                    out = scores_of(i, n)
                    dve.wait_ge(s["c_scores"], i + 1)
                    if br == 0:
                        own.after(dve.tensor_tensor(out, out, m.cmp_mask[:, t, :], ALU.add))
                    else:
                        last = dve.tensor_tensor(out[:, n - P:n], out[:, n - P:n], m.causal, ALU.add)
                        if br == 2 and t >= 4:
                            last = dve.tensor_tensor(out[:, 0:P], out[:, 0:P], m.edge, ALU.add)
                        own.after(last)
                    peak = m.nmax[:, i % 8:i % 8 + 1]
                    wait(dve, "c_exp", i - 7)
                    if br == 0 and t == 0:
                        own.after(dve.tensor_reduce(peak, out, AX.X, ALU.max, negate=True))
                        dve.tensor_scalar(peak, peak, -0.1 * NEG, None, ALU.min).then_inc(s["c_max"], 1)
                    else:
                        dve.tensor_reduce(peak, out, AX.X, ALU.max, negate=True).then_inc(s["c_max"], 1)
                elif what == "T" and on_dve(i):
                    u, first, n = TURNS_C[i]
                    w = min(P, width(u))
                    dve.wait_ge(s["c_turned"], i + 1)
                    wait(dve, "c_pv", values_before(i - 2))
                    dve.tensor_copy(m.pts[i % 3][0:w, 0:P * n], m.banks[0:w, 4 + i % 2, 0:P * n]
                                    ).then_inc(s["c_kept_dve"], 1)
                elif what == "E":
                    t, sums = i, m.sums[i % 2]
                    dve.wait_ge(s["c_exp"], PER_TILE * (t + 1))
                    wait(dve, "c_weighted", t)
                    own.after(dve.tensor_scalar(sums, sums, 1e-30, None, ALU.max))
                    own.after(dve.reciprocal(m.rsc, sums))
                    dve.tensor_tensor(m.rsc.rearrange("p (h g r) -> p h g r", h=4, g=2),
                                      m.rsc.rearrange("p (h g r) -> p h g r", h=4, g=2),
                                      m.gates[:, t, :].rearrange("p (g h r) -> p h g r", g=2, h=4), ALU.mult
                                      ).then_inc(s["c_inverted"], 1)
                    dve.wait_ge(s["c_weighted"], t + 1)
                    if t:
                        dve.wait_ge(s["c_turned"], 1 + [x[0:2] for x in TURNS_C].index(("mix", t - 1)))
                    dve.tensor_reduce(m.osum.rearrange("p (a d) -> p a d", d=HD),
                                      m.oraw.rearrange("p (a r) d -> p a d r", r=3), AX.X, ALU.add
                                      ).then_inc(s["c_osum"], 1)


def stage_mix_out(nc, s, m, io):
    wait = s.wait
    with nc.Block() as block:

        @block.sync
        def _(sp):
            for i in range(NT + 1):
                if i < NT:
                    if i >= 2:
                        sp.wait_ge(s[f"mid_out{i % 2}"], 16 * (i // 2))
                        sp.wait_ge(s["d_h"], i - 1)
                    src = io.xp[i * P:(i + 1) * P, :] if i < TP else io.xs
                    sp.dma_start(m.xr[i % 2][0:rows(i), :], src).then_inc(s[f"d_x{i % 2}"], 16)
                if i >= 1:
                    k = i - 1
                    sp.wait_ge(s["d_mid"], k + 1)
                    sp.dma_start(io.mid[k * P:k * P + rows(k), :], m.xr[k % 2][0:rows(k), :]
                                 ).then_inc(s[f"mid_out{k % 2}"], 16)
            sp.wait_ge(s["mid_out0"], 16 * 5)
            sp.wait_ge(s["mid_out1"], 16 * 4)

        @block.tensor
        def _(pe):
            pe.wait_ge(s["wo_in"], 48)
            for i in range(NT + 1):
                if i < NT:
                    r = rows(i)
                    wait(pe, "d_mid", i - 1)
                    for n in range(2):
                        for k in range(8):
                            last = pe.matmul(m.banks[0:r, 2 * (i % 2) + n, :], m.mixT[:, k, i * P:i * P + r],
                                             m.wo[:, k, 512 * n:512 * n + 512], start=(k == 0), stop=(k == 7))
                    last.then_inc(s["d_mm"], 1)
                if i >= 1:
                    j = i - 1
                    r = rows(j)
                    pe.wait_ge(s["d_h"], j + 1)
                    wait(pe, "d_kept_dve", j - 1)
                    wait(pe, "d_kept_act", j - 1)
                    for k in range(KT):
                        last = pe.transpose(m.banks[:, 4 + 2 * (j % 2) + k // 4, P * (k % 4):P * (k % 4) + r],
                                            m.dh[j % 2][0:r, P * k:P * k + P], m.ident[0:r, 0:r])
                    last.then_inc(s["d_turned"], 1)

        def turned(j, half):
            b = m.banks[:, 4 + 2 * (j % 2) + half, :].rearrange("p (k t) -> p k t", k=4)
            return m.h2T[:, 4 * half:4 * half + 4, j * P:j * P + rows(j)], b[:, :, 0:rows(j)]

        @block.scalar
        def _(act):
            own = Links(act, s, "d_act")
            for i in range(NT + 1):
                if i < NT:
                    r = rows(i)
                    act.wait_ge(s["d_mid"], i + 1)
                    own.after(act.activation(m.dsq[0:r, :], m.xr[i % 2][0:r, :], ACT.Square,
                                             accum_out=m.small[0:r, i:i + 1]))
                    act.activation(m.small[0:r, 16 + i:17 + i], m.small[0:r, i:i + 1], ACT.Sqrt,
                                   bias=m.small[0:r, 64:65], scale=1.0 / DM).then_inc(s["d_rms"], 1)
                if i >= 1:
                    act.wait_ge(s["d_turned"], i)
                    act.activation(*turned(i - 1, 1), ACT.Copy).then_inc(s["d_kept_act"], 1)

        @block.vector
        def _(dve):
            own = Links(dve, s, "d_dve")
            dve.wait_ge(s["ln2_in"], 16)
            for i in range(NT + 1):
                if i < NT:
                    r = rows(i)
                    x = m.xr[i % 2][0:r, :]
                    dve.wait_ge(s[f"d_x{i % 2}"], 16 * (i // 2 + 1))
                    dve.wait_ge(s["d_mm"], i + 1)
                    b = m.banks[0:r, 2 * (i % 2):2 * (i % 2) + 2, :].rearrange("p a n -> p (a n)")
                    dve.tensor_tensor(x, b, x, ALU.add).then_inc(s["d_mid"], 1)
                    dve.wait_ge(s["d_rms"], i + 1)
                    own.after(dve.reciprocal(m.small[0:r, 32 + i:33 + i], m.small[0:r, 16 + i:17 + i]))
                    wait(dve, "d_turned", i - 1)
                    dve.scalar_tensor_tensor(out=m.dh[i % 2][0:r, :], in0=x, scalar=m.small[0:r, 32 + i:33 + i],
                                             in1=m.lnb[0:r, :], op0=ALU.mult, op1=ALU.mult).then_inc(s["d_h"], 1)
                if i >= 1:
                    dve.wait_ge(s["d_turned"], i)
                    dve.tensor_copy(*turned(i - 1, 0)).then_inc(s["d_kept_dve"], 1)


def stage_feed_forward(nc, s, m, io):
    wait = s.wait
    RE, RF = NF // 2, KT // 2
    tok = [slice(TC * q, TC * q + TC) for q in range(3)]
    with nc.Block() as block:

        @block.sync
        def _(sp):
            def load(f, r):
                for k, w in enumerate((io.w_gate, io.w_up)):
                    sp.dma_start(m.wgu[r][:, k, :, :], w[:, :, bass.ds(f * P, P)]).then_inc(s[f"wgu_in{r}"], 16)

            sp.dma_start(m.lnb, io.ln_f.rearrange("(a n) -> a n", a=1).to_broadcast((P, DM))).then_inc(s["lnf_in"], 16)
            load(0, 0)
            load(1, 1)
            with sp.Fori(0, RE - 1) as p:
                for r in range(2):
                    sp.wait_ge(s["e_mm"], p * 6 + 3 * r + 3)
                    load(p * 2 + 2 + r, r)

        @block.tensor
        def _(pe):
            with pe.Fori(0, RE) as p:
                for r in range(2):
                    pe.wait_ge(s[f"wgu_in{r}"], p * 32 + 32)
                    for q in range(3):
                        pe.wait_ge(s["e_product"], p * 6 + 3 * r + q + 1)
                        for k in range(2):
                            for kt in range(KT):
                                last = pe.matmul(m.banks[:, 2 * q + k, 0:TC], m.wgu[r][:, k, kt, :], m.h2T[:, kt, tok[q]],
                                                 start=(kt == 0), stop=(kt == KT - 1))
                        last.then_inc(s["e_mm"], 1)

        @block.scalar
        def _(act):
            with act.Fori(0, RE) as p:
                for r in range(2):
                    for q in range(3):
                        act.wait_ge(s["e_mm"], p * 6 + 3 * r + q + 1)
                        act.wait_ge(s["e_product"], p * 6 + 3 * r + q + 1)
                        act.activation(m.sg[q], m.banks[:, 2 * q, 0:TC], ACT.Silu).then_inc(s["e_silu"], 1)

        @block.vector
        def _(dve):
            dve.sem_inc(s["e_product"], 3)
            with dve.Fori(0, RE) as p:
                for r in range(2):
                    for q in range(3):
                        dve.wait_ge(s["e_silu"], p * 6 + 3 * r + q + 1)
                        dve.tensor_tensor(m.aT[:, bass.ds(p * 2 + r, 1), tok[q]].rearrange("p f t -> p (f t)"),
                                          m.banks[:, 2 * q + 1, 0:TC], m.sg[q], ALU.mult).then_inc(s["e_product"], 1)

    with nc.Block() as block:

        @block.sync
        def _(sp):
            def load(n, r):
                sp.dma_start(m.wd[r], io.w_down[:, :, bass.ds(n * P, P)]).then_inc(s[f"wd_in{r}"], 16)

            load(0, 0)
            load(1, 1)
            with sp.Fori(0, RF - 1) as p:
                for r in range(2):
                    sp.wait_ge(s["f_mm"], p * 6 + 3 * r + 3)
                    load(p * 2 + 2 + r, r)

        @block.tensor
        def _(pe):
            with pe.Fori(0, RF) as p:
                for r in range(2):
                    pe.wait_ge(s[f"wd_in{r}"], p * 16 + 16)
                    for q in range(3):
                        j = 3 * r + q
                        pe.wait_ge(s["f_kept_act" if j % 2 else "f_kept_dve"], p * 3 + j // 2 + 1)
                        for f in range(NF):
                            last = pe.matmul(m.banks[:, j, 0:TC], m.wd[r][:, f, :], m.aT[:, f, tok[q]],
                                             start=(f == 0), stop=(f == NF - 1))
                        last.then_inc(s["f_mm"], 1)

        def out(p, j):
            return m.yT[:, bass.ds(p * 2 + j // 3, 1), tok[j % 3]].rearrange("p k t -> p (k t)"), m.banks[:, j, 0:TC]

        @block.scalar
        def _(act):
            act.sem_inc(s["f_kept_act"], 3)
            with act.Fori(0, RF) as p:
                for j in (1, 3, 5):
                    act.wait_ge(s["f_mm"], p * 6 + j + 1)
                    act.activation(*out(p, j), ACT.Copy).then_inc(s["f_kept_act"], 1)

        @block.vector
        def _(dve):
            dve.sem_inc(s["f_kept_dve"], 3)
            with dve.Fori(0, RF) as p:
                for j in (0, 2, 4):
                    dve.wait_ge(s["f_mm"], p * 6 + j + 1)
                    dve.tensor_copy(*out(p, j)).then_inc(s["f_kept_dve"], 1)


def stage_last_norm(nc, s, m, io):
    wait = s.wait
    with nc.Block() as block:

        @block.sync
        def _(sp):
            for i in range(NT + 1):
                if i < NT:
                    if i >= 3:
                        sp.wait_ge(s[f"y_out{i % 3}"], 16 * (i // 3))
                    sp.dma_start(m.gx[i % 3][0:rows(i), :], io.mid[i * P:i * P + rows(i), :]).then_inc(s[f"g_x{i % 3}"], 16)
                if i >= 1:
                    k = i - 1
                    sp.wait_ge(s["g_y"], k + 1)
                    sp.dma_start(io.yp[k * P:(k + 1) * P, :] if k < TP else io.ys, m.gx[k % 3][0:rows(k), :]
                                 ).then_inc(s[f"y_out{k % 3}"], 16)
            for k in range(3):
                sp.wait_ge(s[f"y_out{k}"], 16 * 3)

        @block.tensor
        def _(pe):
            for i in range(NT):
                r = rows(i)
                wait(pe, "g_sum", i - 3)
                for k in range(KT):
                    last = pe.transpose(m.banks[0:r, 2 * (i % 4) + k // 4, P * (k % 4):P * (k % 4) + P],
                                        m.yT[:, k, i * P:i * P + r], m.ident)
                last.then_inc(s["g_turned"], 1)

        @block.scalar
        def _(act):
            own = Links(act, s, "g_act")
            for i in range(NT):
                r = rows(i)
                act.wait_ge(s["g_sum"], i + 1)
                own.after(act.activation(m.gsq[0:r, :], m.gx[i % 3][0:r, :], ACT.Square, accum_out=m.small[0:r, i:i + 1]))
                act.activation(m.small[0:r, 16 + i:17 + i], m.small[0:r, i:i + 1], ACT.Sqrt,
                               bias=m.small[0:r, 64:65], scale=1.0 / DM).then_inc(s["g_rms"], 1)

        @block.vector
        def _(dve):
            own = Links(dve, s, "g_dve")
            dve.wait_ge(s["lnf_in"], 16)
            for i in range(NT + 1):
                if i < NT:
                    r = rows(i)
                    dve.wait_ge(s[f"g_x{i % 3}"], 16 * (i // 3 + 1))
                    dve.wait_ge(s["g_turned"], i + 1)
                    b = m.banks[0:r, 2 * (i % 4):2 * (i % 4) + 2, :].rearrange("p a n -> p (a n)")
                    dve.tensor_tensor(m.gx[i % 3][0:r, :], b, m.gx[i % 3][0:r, :], ALU.add).then_inc(s["g_sum"], 1)
                if i >= 1:
                    k = i - 1
                    r = rows(k)
                    x = m.gx[k % 3][0:r, :]
                    dve.wait_ge(s["g_rms"], k + 1)
                    own.after(dve.reciprocal(m.small[0:r, 32 + k:33 + k], m.small[0:r, 16 + k:17 + k]))
                    dve.scalar_tensor_tensor(out=x, in0=x, scalar=m.small[0:r, 32 + k:33 + k], in1=m.lnb[0:r, :],
                                             op0=ALU.mult, op1=ALU.mult).then_inc(s["g_y"], 1)


def stage_retention_norm(nc, s, m, io):
    wait = s.wait
    NR = NB_SEQ * 8
    S0, S1, S2 = m.S0[0:NR, :], m.S1[0:NR, :], m.S2[0:NR, :]
    S0v, S1v, S2v = (v.rearrange("p (d e) -> p d e", d=HD) for v in (S0, S1, S2))
    q, k, v, g = (m.R4[0:NR, j, :] for j in range(4))
    o, k8, prod, qs = (m.rsm[0:NR, HD * j:HD * j + HD] for j in range(4))
    qk, ss, rms, rstd = (m.rst[0:NR, 64 + j:65 + j] for j in range(4))
    with nc.Block() as block:

        @block.sync
        def _(sp):
            sp.dma_start(S0, io.state_in).then_inc(s["r_state_in"], 16)
            sp.dma_start(m.R4[0:NR, :, :], io.ret_rows.rearrange("b h j e -> (b h) j e")).then_inc(s["r_rows_in"], 16)
            sp.dma_start(m.gs[0:8, :, :], io.gate_rows.rearrange("b (r n) -> r b n", r=8)).then_inc(s["gs_in"], 16)
            sp.wait_ge(s["r_o"], 1)
            sp.dma_start(io.ret_out.rearrange("b (h e) -> (b h) e", e=HD), o).then_inc(s["r_o_out"], 16)
            sp.wait_ge(s["r_new_state"], 1)
            sp.dma_start(io.state_out, S1).then_inc(s["r_state_out"], 16)
            sp.wait_ge(s["r_o_out"], 16)
            sp.dma_start(m.rrow[0:NB_SEQ, :], io.ret_out).then_inc(s["r_o_in"], 16)
            sp.wait_ge(s["r_state_out"], 16)
            sp.wait_ge(s["gs_in"], 16)

        @block.scalar
        def _(act):
            for hp in range(4):
                act.wait_ge(s["r_sums"], hp + 1)
                act.activation(m.rst[:, 16 * hp:16 * hp + 16], m.rst[:, 16 * hp:16 * hp + 16], ACT.Sqrt,
                               bias=m.small[:, 64:65], scale=1.0 / HD).then_inc(s["r_rms"], 1)
            act.wait_ge(s["r_ssum"], 1)
            act.activation(rms, ss, ACT.Sqrt, bias=m.small[0:NR, 64:65], scale=1.0 / HD).then_inc(s["r_srms"], 1)
            for hp in range(4):
                for half in range(2):
                    act.wait_ge(s["r_turned"], 2 * hp + half + 1)
                    act.activation(m.mixT[:, 4 + hp, 512 * half:512 * half + 512], m.banks[:, 2 * (hp % 2) + half, :],
                                   ACT.Copy).then_inc(s["r_kept"], 1)
            act.wait_ge(s["r_sturned"], 1)
            act.activation(m.mixT[:, 4:8, SEQ:TOK], m.banks[:, 4, 0:32].rearrange("p (k t) -> p k t", k=4),
                           ACT.Copy).then_inc(s["r_skept"], 1)

        @block.gpsimd
        def _(pool):
            for hp in range(4):
                pool.tensor_tensor(m.rsq[:, 1024 * hp:1024 * hp + 1024].rearrange("p (t n) -> p t n", t=TP),
                                   m.oall[hp], m.oall[hp], ALU.mult).then_inc(s["r_sq"], 1)
            pool.wait_ge(s["r_k8"], 1)
            pool.tensor_tensor(S1v, k8.unsqueeze(2).broadcast_to(S1v.shape), v.unsqueeze(1).broadcast_to(S1v.shape),
                               ALU.mult).then_inc(s["r_outer"], 1)
            for hp in range(4):
                heads_o = m.oall[hp].rearrange("p t (h d) -> p (t h) d", h=2)
                pool.wait_ge(s["r_rstd"], hp + 1)
                pool.tensor_tensor(heads_o, heads_o,
                                   m.rst[:, 16 * hp:16 * hp + 16].unsqueeze(2).broadcast_to(heads_o.shape),
                                   ALU.mult).then_inc(s["r_scaled"], 1)
                pool.wait_ge(s["r_scaled"], hp + 1)
                pool.tensor_tensor(m.oall[hp], m.oall[hp], m.gall[hp], ALU.mult).then_inc(s["r_gated"], 1)

        @block.vector
        def _(dve):
            own = Links(dve, s, "r_dve")
            for hp in range(4):
                dve.wait_ge(s["r_sq"], hp + 1)
                dve.tensor_reduce(m.rst[:, 16 * hp:16 * hp + 16],
                                  m.rsq[:, 1024 * hp:1024 * hp + 1024].rearrange("p (t d) -> p t d", d=HD),
                                  AX.X, ALU.add).then_inc(s["r_sums"], 1)
            dve.wait_ge(s["r_rows_in"], 16)
            dve.tensor_scalar(k8, k, 0.125, None, ALU.mult).then_inc(s["r_k8"], 1)
            dve.wait_ge(s["r_k8"], 1)
            own.after(dve.tensor_tensor(prod, q, k8, ALU.mult))
            own.after(dve.tensor_reduce(qk, prod, AX.X, ALU.add))
            dve.tensor_scalar(o, v, qk, None, ALU.mult)
            for hp in range(4):
                dve.wait_ge(s["r_rms"], hp + 1)
                dve.reciprocal(m.rst[:, 16 * hp:16 * hp + 16], m.rst[:, 16 * hp:16 * hp + 16]).then_inc(s["r_rstd"], 1)
            dve.wait_ge(s["r_state_in"], 16)
            own.after(dve.tensor_tensor(S2v, S0v.rearrange("p d e -> p e d"), q.unsqueeze(1).broadcast_to(S2v.shape),
                                        ALU.mult))
            own.after(dve.tensor_reduce(qs, S2v, AX.X, ALU.add))
            own.after(dve.scalar_tensor_tensor(out=o, in0=qs, scalar=m.gone[0:NR, :], in1=o, op0=ALU.mult, op1=ALU.add))
            own.after(dve.tensor_tensor(prod, o, o, ALU.mult))
            dve.tensor_reduce(ss, prod, AX.X, ALU.add).then_inc(s["r_ssum"], 1)
            dve.wait_ge(s["r_outer"], 1)
            dve.scalar_tensor_tensor(out=S1, in0=S0, scalar=m.gone[0:NR, :], in1=S1, op0=ALU.mult,
                                     op1=ALU.add).then_inc(s["r_new_state"], 1)
            dve.wait_ge(s["r_srms"], 1)
            own.after(dve.reciprocal(rstd, rms))
            dve.scalar_tensor_tensor(out=o, in0=o, scalar=rstd, in1=g, op0=ALU.mult, op1=ALU.mult).then_inc(s["r_o"], 1)

        @block.tensor
        def _(pe):
            for hp in range(4):
                pe.wait_ge(s["r_gated"], hp + 1)
                for half in range(2):
                    if hp >= 2:
                        pe.wait_ge(s["r_kept"], 2 * (hp - 2) + half + 1)
                    for i in range(4):
                        last = pe.transpose(m.banks[:, 2 * (hp % 2) + half, P * i:P * i + P],
                                            m.oall[hp][:, 4 * half + i, :], m.ident)
                    last.then_inc(s["r_turned"], 1)
            pe.wait_ge(s["r_o_in"], 16)
            for i in range(4):
                last = pe.transpose(m.banks[:, 4, NB_SEQ * i:NB_SEQ * i + NB_SEQ],
                                    m.rrow[0:NB_SEQ, P * i:P * i + P], m.ident[0:NB_SEQ, 0:NB_SEQ])
            last.then_inc(s["r_sturned"], 1)

def build(nc, x_prompt, x_sample, cache_kv, cache_win, state_ret, page_table, ln1, w_in, cmp_pos_k, cmp_w1_k,
          cmp_w2_k, cmp_pos_v, cmp_w1_v, cmp_w2_v, w_out, ln2, w_gate, w_up, w_down, ln_f, const,
          y_prompt, y_sample, kv_prompt, kv_sample, win_prompt, win_sample, ret_prompt, ret_sample):
    io = Named()
    io.xp, io.xs = x_prompt[0], x_sample.rearrange("b s d -> (b s) d")
    io.const, io.ln1, io.ln2, io.ln_f = const, ln1, ln2, ln_f
    io.w_in = w_in[0].rearrange("(k p) n -> p k n", p=P)
    io.pool = cache_kv[0].rearrange("n (c t) s g d -> n c t (s g d)", t=CH)
    io.kvp = kv_prompt[0, 0].rearrange("t s g d -> t (s g d)")
    io.kvs = kv_sample[0].rearrange("b t s g d -> (b t) (s g d)")
    io.winp = win_prompt[0, 0].rearrange("t s g d -> t (s g d)")
    io.cwin = cache_win[0].rearrange("b t s g d -> b t (s g d)")
    io.wins = win_sample[0].rearrange("b t s g d -> b t (s g d)")
    io.retp = ret_prompt[0, 0].rearrange("(a h) d e -> a (h d) e", h=2)
    io.state_in = state_ret[0].rearrange("b h d e -> (b h) (d e)")
    io.state_out = ret_sample[0].rearrange("b h d e -> (b h) (d e)")
    io.table = page_table.rearrange("b n -> (b n)").rearrange("(a n) -> a n", a=1)
    io.w1 = [w[0].rearrange("(k p) n -> p k n", p=P) for w in (cmp_w1_k, cmp_w1_v)]
    io.w2 = [w[0].rearrange("(m p) n -> p m n", p=P) for w in (cmp_w2_k, cmp_w2_v)]
    io.pos = [w[0].rearrange("(k t) d -> (t d) k", t=2) for w in (cmp_pos_k, cmp_pos_v)]
    io.w_out = w_out[0]
    io.w_gate, io.w_up = (w[0].rearrange("(k p) n -> p k n", p=P) for w in (w_gate, w_up))
    io.w_down = w_down[0].rearrange("(f p) n -> p f n", p=P)
    io.yp, io.ys = y_prompt[0], y_sample.rearrange("b s d -> (b s) d")
    io.mid = nc.dram_tensor("mid", (TOK, DM), F32).ap()
    io.gate_rows = nc.dram_tensor("gate_rows", (NB_SEQ, GW), F32).ap()
    io.ret_rows = nc.dram_tensor("ret_rows", (NB_SEQ, 8, 4, HD), F32).ap()
    io.ret_out = nc.dram_tensor("ret_out", (NB_SEQ, 512), F32).ap()
    with ExitStack() as ctx:
        s = Semaphores(nc, ctx)
        m = place_memory(nc, ctx)
        for stage in STAGES:
            stage(nc, s, m, io)


STAGES = [stage_project, stage_retention_norm, stage_sequences, stage_attention, stage_mix_out, stage_feed_forward,
          stage_last_norm]

_INS = ['x_prompt', 'x_sample', 'cache_kv', 'cache_win', 'state_ret', 'page_table', 'ln1', 'w_in', 'cmp_pos_k',
        'cmp_w1_k', 'cmp_w2_k', 'cmp_pos_v', 'cmp_w1_v', 'cmp_w2_v', 'w_out', 'ln2', 'w_gate', 'w_up', 'w_down',
        'ln_f']
_OUTS = [(1, SEQ, DM), (NB_SEQ, 1, DM), (1, 1, SEQ, 4, 2, HD), (1, NB_SEQ, 1, 4, 2, HD), (1, 1, WIN, 2, 2, HD),
         (1, NB_SEQ, WIN, 2, 2, HD), (1, 1, 8, HD, HD), (1, NB_SEQ, 8, HD, HD)]


def kernel(**inputs):
    import concourse.bacc as bacc
    from concourse.bass_utils import run_bass_kernel_spmd as run

    arrays = {f"in_{n}": np.ascontiguousarray(inputs[n]) for n in _INS}
    arrays["in_const"] = constants()
    nc = bacc.Bacc("TRN2", target_bir_lowering=False, num_devices=1)
    args = [nc.dram_tensor(n, a.shape, mybir.dt.from_np(a.dtype), kind="ExternalInput").ap() for n, a in arrays.items()]
    args += [nc.dram_tensor(f"out_{i}", s, F32, kind="ExternalOutput").ap() for i, s in enumerate(_OUTS)]
    build(nc, *args)
    r = run(nc, [arrays], core_ids=[0])
    return tuple(r.results[0][f"out_{i}"] for i in range(len(_OUTS)))
```

```python
from contextlib import ExitStack

import concourse.bass as bass
import numpy as np
from concourse import mybir

F32 = mybir.dt.float32
F32R = mybir.dt.float32r
BF16 = mybir.dt.bfloat16
I32 = mybir.dt.int32
ALU = mybir.AluOpType
ACT = mybir.ActivationFunctionType
AX = mybir.AxisListType

P = 128
DM = 1024
KT = DM // P
SEQ = 1024
NB_SEQ = 8
PAST = 2048
PAGE = 128
NPOOL = 160
HD = 64
NT = 9
TP = SEQ // P
TOK = SEQ + NB_SEQ
FF = 2816
NF = FF // P
TC = TOK // 3
WIN = 512
EPS = 1e-6
CH = 16
NEG = -1e30
NSEL = 33
NRANK = 30
TOP = 13

QW, KVW, GW, RW = 512, 768, 24, 512
KV0 = QW
R0 = QW + KVW + GW
CHUNKS = [("ret", i) for i in range(4)] + ["kv", "win", "q"]
NCH = len(CHUNKS)
WIDTH = [512] * 5 + [256 + GW, 512]
NI = NCH * NT
NRAW = 5
NSLOT = 6
FP = 8
PARTS = [(0, 8), (8, 7), (15, 7)]
CORE = P + DM + 256 + 8 * TOK + NSLOT * DM
KEPT = 8 * SEQ + 64 + NT * GW + 8 + 24 + 192
WORDS = CORE + 2 * 8 * TOK + 2 * FP * TOK + 4 * DM

CONST = {}


def constants():
    lg = np.log((1.0 - 2.0 ** (-5.0 - np.arange(8, dtype=np.float32))).astype(np.float32)).astype(np.float64)
    parts = []

    def put(name, a):
        a = np.asarray(a, np.float64).reshape(P, -1).astype(np.float32)
        CONST[name] = (sum(x.shape[1] for x in parts), a.shape[1])
        parts.append(a)

    p = np.arange(P)
    put("ident", np.eye(P))
    inv = (1.0 / (np.float32(10000.0) ** (np.arange(32, dtype=np.float32) / np.float32(32)))).astype(np.float32)
    pos = np.stack([i * P + p if i < TP else np.full(P, PAST) for i in range(NT)], 1).astype(np.float32)
    ang = (pos[:, :, None] * inv).astype(np.float32).astype(np.float64)
    put("rope", np.stack([np.cos(ang), -np.sin(ang), np.sin(ang)], 2))
    i = np.arange(P)
    diff = i[None, :] - p[:, None]
    put("dec", np.stack([np.where(diff >= 0, np.exp(np.maximum(diff, 0) * lg[h]), 0) * 0.125 for h in range(8)], 1))
    put("qdec", np.stack([np.stack([np.exp((i + 1) * lg[2 * hp + (d >= HD)]) for d in p]) for hp in range(4)], 1))
    put("kdec", np.stack([np.exp((P - 1 - p) * lg[h]) * 0.125 for h in range(8)], 1))
    put("gchunk", np.stack([np.exp(P * lg[2 * hp + (p >= HD)]) for hp in range(4)], 1))
    put("gone", np.exp(lg[p % 8]))
    put("causal", np.where(i[None, :] <= p[:, None], 0, NEG))
    put("edge", np.where(i[None, :] > p[:, None], 0, NEG))
    n = np.arange(63)
    put("cmp", np.stack([np.where(n[None, :] * CH + 31 <= t * P + p[:, None], 0, NEG) for t in range(TP)], 1))
    r = np.arange(NRANK)
    put("tie", np.broadcast_to((r[None, :] < r[:, None]).astype(float), (P, NRANK, NRANK)))
    put("group", np.where((p[:, None] // 4 == np.arange(8)[None, :] // 4), 1.0, 0.0))
    return np.ascontiguousarray(np.concatenate(parts, 1))


NCONST = constants().shape[1]
N_EARLY = CONST["causal"][0] - P
N_LATE = CONST["kdec"][0]



class Named:
    pass


class Semaphores:

    def __init__(self, nc, ctx):
        self.nc, self.ctx, self.by_name, self.own_counts = nc, ctx, {}, {}

    def __getitem__(self, name):
        if name not in self.by_name:
            self.by_name[name] = self.ctx.enter_context(self.nc.semaphore(name))
        return self.by_name[name]

    def wait(self, engine, name, value):
        if value > 0:
            engine.wait_ge(self[name], value)


class Links:

    def __init__(self, engine, s, name):
        self.engine, self.sem, self.counts, self.name = engine, s[name], s.own_counts, name

    def after(self, instruction):
        self.counts[self.name] = self.counts.get(self.name, 0) + 1
        instruction.then_inc(self.sem, 1)
        self.engine.wait_ge(self.sem, self.counts[self.name])


class Room:

    def __init__(self, arena, start):
        self.arena, self.at = arena, start

    def __call__(self, n):
        v = self.arena[:, self.at:self.at + n]
        self.at += n
        assert self.at <= self.arena.shape[1], self.at
        return v


def rows(t):
    return P if t < TP else NB_SEQ


def place_core(nc, ctx):
    core = ctx.enter_context(nc.sbuf_tensor("core", [P, CORE], F32))
    m = Named()
    m.banks = ctx.enter_context(nc.psum_tensor("banks", [P, 8, 512], F32))
    room = Room(core, 0)
    m.ident = room(P)
    m.lnb = room(DM)
    m.small = room(256)
    m.mixT = room(8 * TOK).rearrange("p (k t) -> p k t", k=8)
    m.pool = room(NSLOT * DM)
    m.slot = [m.pool[:, DM * i:DM * i + DM] for i in range(NSLOT)]
    return m


def place_constants(m, cst, start):
    def const_of(name):
        at, n = CONST[name]
        return cst[:, at - start:at - start + n] if start <= at and at + n <= start + cst.shape[1] else None

    m.cst = cst
    m.kdec, m.gchunk, m.gone = const_of("kdec"), const_of("gchunk"), const_of("gone")
    m.causal, m.edge, m.group = const_of("causal"), const_of("edge"), const_of("group")
    if const_of("rope") is not None:
        m.rope = const_of("rope").rearrange("p (t s d) -> p t s d", t=NT, s=3)
    if const_of("dec") is not None:
        m.dec = const_of("dec").rearrange("p (h i) -> p h i", h=8)
        m.qdec = const_of("qdec").rearrange("p (h i) -> p h i", h=4)
    if const_of("cmp") is not None:
        m.cmp_mask = const_of("cmp").rearrange("p (t n) -> p t n", t=TP)
        m.tie = const_of("tie").rearrange("p (j i) -> p j i", j=NRANK)


def place_hidden(nc, ctx, m):
    halves = ctx.enter_context(nc.sbuf_tensor("hidden", [P, 16 * TOK + 16 * 512], F32R))
    room = Room(halves, 0)
    m.hT = [room(8 * TOK).rearrange("p (k t) -> p k t", k=8) for _ in range(2)]
    m.wk = [[room(512) for _ in range(2)] for _ in range(KT)]
    m.xt, m.sq = m.slot[0:2], m.slot[2]
    m.raw = [m.pool[:, 3584 + 512 * i:4096 + 512 * i] for i in range(NRAW)]
    m.oall = [m.mixT[:, 4 + i, 0:SEQ].rearrange("p (t n) -> p t n", t=TP) for i in range(4)]
    m.gall = [m.mixT[:, i, 0:SEQ].rearrange("p (t n) -> p t n", t=TP) for i in range(4)]


def place_retention(nc, ctx, m):
    n = N_EARLY + 8 * 512 + 4 * 512 + 3840 - 2048
    a = Room(ctx.enter_context(nc.sbuf_tensor("retention", [P, n], F32, side="right")), 0)
    place_constants(m, a(N_EARLY), P)
    m.wstage = [(a(7 * 512), a(512)), (m.pool[:, 0:7 * 512], m.lnb[:, 0:512])]
    m.t1, m.t2 = [a(512) for _ in range(2)], [a(512) for _ in range(2)]
    m.rT = [a(256).rearrange("p (a t) -> p a t", a=2) for _ in range(2)]
    m.qd = [a(128) for _ in range(2)]
    m.kd = [a(128) for _ in range(2)]
    m.att = [a(256).rearrange("p (a t) -> p a t", a=2) for _ in range(2)]
    m.state = [a(64) for _ in range(4)]


def place_kept(nc, ctx, m):
    room = Room(ctx.enter_context(nc.sbuf_tensor("kept", [P, KEPT], F32,
                                                 side="right")), 0)
    m.qT = room(4 * SEQ).rearrange("p (h t) -> p h t", h=4)
    m.qbd = room(64).rearrange("p (b r) -> p b r", b=8)
    m.kselT, m.kwinT = room(SEQ), room(SEQ)
    m.vsel = room(SEQ).rearrange("p (t n) -> p t n", t=TP)
    m.vwin = room(SEQ).rearrange("p (t n) -> p t n", t=TP)
    m.gates = room(NT * GW).rearrange("p (t n) -> p t n", t=NT)
    m.ksnew = room(8)
    m.gs = room(24).rearrange("p (b n) -> p b n", b=8)
    m.kcbP, m.vcbP = room(64), room(128)


def place_keys(nc, ctx, m):
    n = CONST["rope"][1]
    a = Room(ctx.enter_context(nc.sbuf_tensor("keys", [P, n + 4 * 512], F32, side="right")), 0)
    place_constants(m, a(n), P)
    m.t1, m.t2 = [a(512) for _ in range(2)], [a(512) for _ in range(2)]
    m.qp = [m.lnb[:, 512 * i:512 * i + 512] for i in range(2)]


def place_mixer(nc, ctx, m):
    arena = ctx.enter_context(nc.sbuf_tensor("arena", [P, WORDS - CORE - KEPT], F32))
    room = Room(arena, 0)
    place_constants(m, room(NCONST - N_LATE), N_LATE)
    m.identb, m.causalb, m.edgeb = (room(P // 2).bitcast(BF16) for _ in range(3))
    m.cmpb16 = room(TP * 32).bitcast(BF16).rearrange("p (t n) -> p t n", t=TP)[:, :, 0:63]
    after_const = room.at

    b = Room(arena, after_const)
    w1v = b(4096)
    m.cmpg = b(4096).rearrange("p (v g t d) -> p v g t d", v=2, g=2, t=CH)
    sel = b(4096)
    m.selk, m.selv = (sel[:, 2048 * i:2048 * i + 2048].rearrange("p (t n) -> p t n", t=CH) for i in range(2))
    w1k = b(4096)
    m.w1 = [w.rearrange("p (k n) -> p k n", k=16) for w in (w1k, w1v)]
    m.XT = b(2048).rearrange("p (j g c) -> p j g c", j=8, g=2)
    scores = b(2048 + 2688)
    m.kselb, m.SR = scores[:, 0:2048], scores[:, 2048:]
    m.w2 = [b(128).rearrange("p (m n) -> p m n", m=2) for _ in range(2)]
    m.posT = [b(16) for _ in range(2)]
    m.cbias = b(4)
    m.pages = b(NB_SEQ * PAST // PAGE).bitcast(I32)
    x = Room(m.pool, 0)
    m.cmpb = x(4096).rearrange("p (t n) -> p t n", t=CH)
    m.wink, m.winv = (x(512).rearrange("p (t n) -> p t n", t=4) for _ in range(2))
    m.kwb = x(512)
    m.rrow = x(512)
    m.G = [b(508).rearrange("p (m n) -> p m n", m=2) for i in range(2)]
    m.brow = b(256)
    m.osm = b(128)
    m.cg = m.mixT[:, 1, 0:900].rearrange("p (j i) -> p j i", j=NRANK)
    m.ce = m.mixT[:, 2, 0:900].rearrange("p (j i) -> p j i", j=NRANK)
    x = Room(m.lnb, 0)
    m.kcb, m.vcb = [x(128), x(128)], [x(128), x(128)]
    m.PT = x(168)
    m.bst, m.imp, m.blkm, m.pcn = x(40), x(32), x(32), x(128)
    m.rst = x(72)
    m.S0, m.S2, m.rsq = scores[:, 0:4096], sel, sel[:, 0:1024]
    m.rsm = m.pool[:, 4096 + 512:4096 + 1024]
    m.R4 = m.kwb[:, 0:256].rearrange("p (j e) -> p j e", j=4)

    c = Room(arena, after_const)
    m.prob = [c(1024) for _ in range(4)]
    m.qz = [c(8 * P).rearrange("p (h g t) -> p h g t", h=4, g=2) for _ in range(2)]
    m.pts = [c(512) for _ in range(3)]
    m.oraw = [c(24 * HD).rearrange("p (u d) -> p u d", u=24) for _ in range(2)]
    m.osum = c(512)
    m.sums, m.rsc, m.nmax = [c(24), c(24)], c(24), c(8)


def place_feed_forward(nc, ctx, m):
    halves = ctx.enter_context(nc.sbuf_tensor("halves", [P, WORDS - CORE], F32R))
    room = Room(halves, 0)
    m.h2T = [room(8 * TOK).rearrange("p (k t) -> p k t", k=8) for _ in range(2)]
    start = room.at
    m.aT = [room(FP * TOK).rearrange("p (f t) -> p f t", f=FP) for _ in range(2)]
    m.wring = [[room(DM) for _ in range(2)] for _ in range(2)]
    d = Room(halves, start)
    m.wo = [d(8 * DM).rearrange("p (k n) -> p k n", k=8) for _ in range(2)]
    m.mix = [[x.rearrange("p (k t) -> p k t", k=8) for x in pair] for pair in m.wring]
    m.xr, m.dh = m.slot[2:4], m.slot[4:6]
    late = Room(halves, 0)
    m.wlast = m.wring + [[late(DM) for _ in range(2)] for _ in range(KT - 2)]
    assert late.at <= start
    m.wstage = m.slot[0:2]
    m.sg = [m.pool[:, 2 * DM + TC * q:2 * DM + TC * q + TC] for q in range(3)]
    m.yT = m.mixT
    m.gx = [m.slot[i] for i in (4, 5, 2, 3)]
    m.gsq = m.slot[0]

def is_ret(n):
    return 0 <= n < NI and isinstance(CHUNKS[n // NT], tuple) and n % NT < TP


def turns(n):
    if not 0 <= n < NI:
        return False
    kind = CHUNKS[n // NT]
    return kind in ("kv", "q") or (kind == "win" and n % NT < TP) or is_ret(n)


def turns_before(n):
    return sum(turns(k) for k in range(n))


def ret_before(n):
    return sum(is_ret(k) for k in range(n))


def stored(n):
    kind, t = CHUNKS[n // NT], n % NT
    if kind == "kv":
        return 1
    if kind == "win":
        return int(t >= TP - WIN // P)
    return 2 if isinstance(kind, tuple) and t == TP else 0


def weight_loads(ch):
    return sum(8 if isinstance(kind, tuple) else 2 for kind in CHUNKS[:ch + 1])


def stored_before(n):
    return sum(stored(k) for k in range(n % NRAW, n, NRAW))


def vkeep_before(n):
    return sum(1 for k in range(n) if CHUNKS[k // NT] in ("kv", "win") and k % NT < TP)


def heads(kind, ap):
    if kind == "kv":
        return ap[:, 0:512].rearrange("p (s v h d) -> p s v h d", s=2, v=2, h=2)[:, :, 0, :, :]
    n = 128 if kind == "win" else 512 if kind == "q" else 256
    return ap[:, 0:n].rearrange("p (s h d) -> p s h d", s=1, d=HD)


def split_products(pe, out, left, right, first, last):
    for i, (a, b) in enumerate(((0, 0), (1, 0), (0, 1))):
        done = pe.matmul(out, left[a], right[b], start=(first and i == 0), stop=(last and i == 2))
    return done


def round_to_hi(act, hi, x):
    return act.activation(hi, x, ACT.Copy)


def rest_to_lo(engine, lo, x, hi):
    return engine.tensor_tensor(lo, x, hi.bitcast(F32), ALU.subtract)


TURN_STEPS = (3, 6)


def stage_project(nc, s, m, io, first, end):
    wait = s.wait
    n0, n1 = first * NT, end * NT
    steps = range(n0, n1 + 3)

    def here(n):
        return n0 <= n < n1

    def turned_half(i, half):
        b = m.banks[:, 0, :].rearrange("p (k t) -> p k t", k=4)[:, :, 0:rows(i)]
        return b, [v[:, 4 * half:4 * half + 4, i * P:i * P + rows(i)] for v in m.hT]

    def staged(ch, k):
        main, rest = m.wstage[ch >= 4]
        return main[:, 512 * k:512 * k + WIDTH[ch]] if k < KT - 1 else rest[:, 0:WIDTH[ch]]

    with nc.Block() as block:

        @block.sync
        def _(sp):
            def load_chunk(ch):
                wait(sp, "aw_lo", KT * ch)
                kind = CHUNKS[ch]
                main, rest = m.wstage[ch >= 4]
                for k0, k1, dst in ((0, KT - 1, main), (KT - 1, KT, rest)):
                    dst = dst.rearrange("p (k n) -> p k n", k=k1 - k0)
                    if isinstance(kind, tuple):
                        for j in range(4):
                            at = R0 + RW * j + P * kind[1]
                            sp.dma_start(dst[:, :, P * j:P * j + P], io.w_in[:, k0:k1, at:at + P]).then_inc(s["aw_in"], 16)
                    else:
                        at = {"kv": KV0, "win": KV0 + 512, "q": 0}[kind]
                        sp.dma_start(dst[:, :, 0:WIDTH[ch]], io.w_in[:, k0:k1, at:at + WIDTH[ch]]).then_inc(s["aw_in"], 16)

            def load_x(i):
                src = io.xp[i * P:(i + 1) * P, :] if i < TP else io.xs
                sp.dma_start(m.xt[i % 2][0:rows(i), :], src).then_inc(s[f"x_in{i % 2}"], 16)

            if first == 0:
                load_x(0)
                sp.dma_start(m.ident, io.const[:, 0:P]).then_inc(s["ident_in"], 16)
                sp.dma_start(m.lnb, io.ln1[0:1, :].to_broadcast((P, DM))).then_inc(s["ln1_in"], 16)
                load_x(1)
                load_chunk(0)
                sp.dma_start(m.cst, io.const[:, P:P + N_EARLY]).then_inc(s["const_in"], 16)
                for i in range(2, NT):
                    sp.wait_ge(s["turned"], 2 * i - 2)
                    load_x(i)
                    if i == 3:
                        load_chunk(1)
            else:
                sp.dma_start(m.cst, io.const[:, P:P + m.cst.shape[1]]).then_inc(s["const_in"], 16)
            for n in range(n0, n1):
                kind, ch, t = CHUNKS[n // NT], n // NT, n % NT
                if t == 1 and ch + 1 < NCH and ch:
                    load_chunk(ch + 1)
                if n == NT + 5:
                    sp.dma_start(io.wins[:, 0:WIN - 1, :], io.cwin[:, 1:WIN, :]).then_inc(s["rows_out"], 16)
                if n == NI - 5:
                    for k in range(NRAW):
                        wait(sp, f"slot_out{k}", 16 * stored_before(NI + (k - NI) % NRAW))
                    sp.wait_ge(s["aw_lo"], KT * NCH)
                    load_prompt_rows(sp, s, io, m.pool[0:64, 0:256 * EARLY_ROWS], 0, EARLY_ROWS, "cmp_early")
                if not stored(n):
                    continue
                slot, out = m.raw[n % NRAW], s[f"slot_out{n % NRAW}"]
                sp.wait_ge(s["roped"], n + 1)
                if kind == "kv":
                    dst = io.kvp[t * P:(t + 1) * P, :] if t < TP else io.kvs
                    sp.dma_start(dst, slot[0:rows(t), :]).then_inc(out, 16)
                elif kind == "win":
                    at = (t - TP + WIN // P) * P
                    dst = io.winp[at:at + P, :] if t < TP else io.wins[:, WIN - 1, :]
                    sp.dma_start(dst, slot[0:rows(t), 0:256]).then_inc(out, 16)
                else:
                    src = slot[0:NB_SEQ, :].rearrange("b (j h e) -> b h j e", j=4, h=2)
                    for h2 in range(2):
                        sp.dma_start(io.ret_rows[:, 2 * kind[1] + h2, :, :], src[:, h2, :, :]).then_inc(out, 16)
            if first == 0:
                for hp in range(4):
                    sp.wait_ge(s["state_done"], TP * (hp + 1))
                    sp.dma_start(io.retp[hp], m.state[hp]).then_inc(s["state_out"], 16)
                sp.wait_ge(s["state_out"], 64)
            else:
                sp.wait_ge(s["gate_done"], NT)
                sp.dma_start(io.gate_rows, m.gates[0:NB_SEQ, TP, :]).then_inc(s["rows_out"], 16)
                sp.wait_ge(s["rows_out"], 32)

        @block.scalar
        def _(act):
            own = Links(act, s, "own_act")

            def norm(i):
                act.wait_ge(s[f"x_in{i % 2}"], 16 * (i // 2 + 1))
                r = rows(i)
                own.after(act.activation(m.sq[0:r, :], m.xt[i % 2][0:r, :], ACT.Square,
                                         accum_out=m.small[0:r, i:i + 1]))
                wait(act, "a_dve_const", 1)
                act.activation(m.small[0:r, 16 + i:17 + i], m.small[0:r, i:i + 1], ACT.Sqrt,
                               bias=m.small[0:r, 64:65], scale=1.0 / DM).then_inc(s["rms_done"], 1)

            def hidden_hi(i):
                for half in range(2):
                    act.wait_ge(s["turned"], 2 * i + half + 1)
                    b, (hi, _) = turned_half(i, half)
                    round_to_hi(act, hi, b).then_inc(s["hT_hi"], 1)

            def weights_hi(ch, k):
                act.wait_ge(s["aw_in"], 16 * weight_loads(ch))
                round_to_hi(act, m.wk[k][0][:, 0:WIDTH[ch]], staged(ch, k)).then_inc(s["aw_hi"], 1)

            if first == 0:
                norm(0)
                hidden_hi(0)
                norm(1)
            for k in range(KT):
                weights_hi(first, k)
            for n in range(n0, n1):
                kind, ch, t = CHUNKS[n // NT], n // NT, n % NT
                r = rows(t)
                if n + 2 < NT:
                    norm(n + 2)
                if n == NT:
                    act.wait_ge(s["gates_kept"], NT)
                    act.activation(m.gall[0][:, 0:NT - 2, :], m.gall[0][:, 0:NT - 2, :], ACT.Silu
                                   ).then_inc(s["gates_late"], 1)
                if n + 1 < NT:
                    hidden_hi(n + 1)
                if t == NT - 1 and ch + 1 < end:
                    for k in range(KT):
                        if k < KT - 1:
                            act.wait_ge(s["w_used"], (KT - 1) * (ch - (ch >= 4)) + k + 1)
                        else:
                            act.wait_ge(s["proj_done"], n + 1)
                        weights_hi(ch + 1, k)
                slot, src = m.raw[n % NRAW], m.banks[:, 6 + n % 2, :]
                k = n - NRAW
                if k >= 0:
                    act.wait_ge(s["roped"], k + 1)
                    wait(act, "tturned", turns_before(k + 1))
                    wait(act, "vkept", vkeep_before(k + 1))
                    wait(act, "o_done", ret_before(k + 1))
                    wait(act, f"slot_out{n % NRAW}", 16 * stored_before(n))
                act.wait_ge(s["proj_done"], n + 1)
                if kind == "win":
                    act.activation(m.gates[0:r, t, :], src[0:r, 256:280], ACT.Sigmoid).then_inc(s["gate_done"], 1)
                    act.activation(slot[0:r, 0:256], src[0:r, 0:256], ACT.Copy).then_inc(s["raw_done"], 1)
                elif isinstance(kind, tuple):
                    dst = m.gall[kind[1]][:, t, :] if t < TP else slot[0:r, 384:512]
                    act.activation(dst, src[0:r, 384:512], ACT.Copy if n + 2 < NT else ACT.Silu).then_inc(s["gates_kept"], 1)
                    act.activation(slot[0:r, 0:384], src[0:r, 0:384], ACT.Copy).then_inc(s["raw_done"], 1)
                else:
                    act.activation(slot[0:r, :], src[0:r, :], ACT.Copy).then_inc(s["raw_done"], 1)

        @block.gpsimd
        def _(pool):
            pool.wait_ge(s["const_in"], 16 if first == 0 else 32)
            for n in steps:
                if n < n1:
                    kind, t = CHUNKS[n // NT], n % NT
                    r = rows(t)
                    slot = m.raw[n % NRAW][0:r, :]
                    x = heads(kind, slot).rearrange("p s h (w d) -> p s (h w) d", w=2)
                    y = heads(kind, m.t1[n % 2][0:r, :]).rearrange("p s h (w d) -> p s (h w) d", w=2)
                    cos = m.rope[0:r, t, 0:1, :].unsqueeze(1).broadcast_to(x.shape)
                    pool.wait_ge(s["raw_done"], n + 1)
                    wait(pool, "roped", n - 1)
                    pool.tensor_tensor(y, x, cos, ALU.mult).then_inc(s["cos_done"], 1)
                    if kind in ("kv", "win") and t < TP:
                        dst, at = (m.vsel, 384) if kind == "kv" else (m.vwin, 128)
                        pool.tensor_copy(dst[:, t, :], slot[:, at:at + 128]).then_inc(s["vkept"], 1)
                k = n - 2
                if here(k) and is_ret(k):
                    hp = CHUNKS[k // NT][1]
                    pool.wait_ge(s["roped"], k + 1)
                    wait(pool, "o_done", ret_before(k) - 1)
                    pool.tensor_tensor(m.kd[ret_before(k) % 2].rearrange("p (h d) -> p h d", h=2),
                                       m.raw[k % NRAW][:, 128:256].rearrange("p (h d) -> p h d", h=2),
                                       m.kdec[:, 2 * hp:2 * hp + 2].unsqueeze(2).broadcast_to((P, 2, HD)),
                                       ALU.mult).then_inc(s["kd_done"], 1)

        @block.vector
        def _(dve):
            own = Links(dve, s, "own_dve")
            def norm(i):
                r = rows(i)
                dve.wait_ge(s["rms_done"], i + 1)
                own.after(dve.reciprocal(m.small[0:r, 32 + i:33 + i], m.small[0:r, 16 + i:17 + i]))
                x = m.xt[i % 2][0:r, :]
                dve.scalar_tensor_tensor(out=x, in0=x, scalar=m.small[0:r, 32 + i:33 + i], in1=m.lnb[0:r, :],
                                         op0=ALU.mult, op1=ALU.mult).then_inc(s["h_done"], 1)

            def hidden_lo(i):
                for half in range(2):
                    dve.wait_ge(s["hT_hi"], 2 * i + half + 1)
                    b, (hi, lo) = turned_half(i, half)
                    rest_to_lo(dve, lo, b, hi).then_inc(s["hT_lo"], 1)

            def weights_lo(ch, k):
                dve.wait_ge(s["aw_hi"], KT * ch + k + 1)
                n = WIDTH[ch]
                rest_to_lo(dve, m.wk[k][1][:, 0:n], staged(ch, k), m.wk[k][0][:, 0:n]).then_inc(s["aw_lo"], 1)

            if first == 0:
                dve.memset(m.small[:, 64:65], EPS).then_inc(s["a_dve_const"], 1)
                dve.wait_ge(s["ln1_in"], 16)
                norm(0)
                hidden_lo(0)
            else:
                own.after(dve.memset(m.qbd, 0.0))
            if first == 0:
                norm(1)
            for k in range(KT):
                weights_lo(first, k)
            dve.wait_ge(s["const_in"], 16 if first == 0 else 32)
            for n in steps:
                if n < n1:
                    kind, ch, t = CHUNKS[n // NT], n // NT, n % NT
                    r = rows(t)
                    if n + 2 < NT:
                        norm(n + 2)
                    if n + 1 < NT:
                        hidden_lo(n + 1)
                    if t == NT - 1 and ch + 1 < end:
                        for k in range(KT):
                            weights_lo(ch + 1, k)
                    slot = m.raw[n % NRAW][0:r, :]
                    x, y = heads(kind, slot), heads(kind, m.t2[n % 2][0:r, :])
                    c = heads(kind, m.t1[n % 2][0:r, :])
                    dve.wait_ge(s["raw_done"], n + 1)
                    wait(dve, "roped", n - 1)
                    shape = x[:, :, :, 0:32].shape
                    for half in range(2):
                        sin = m.rope[0:r, t, 1 + half:2 + half, :].unsqueeze(1).broadcast_to(shape)
                        own_in = dve.tensor_tensor(y[:, :, :, 32 * half:32 * half + 32],
                                                   x[:, :, :, 32 - 32 * half:64 - 32 * half], sin, ALU.mult)
                    own.after(own_in)
                    dve.wait_ge(s["cos_done"], n + 1)
                    if kind == "q":
                        wait(dve, "tturned", turns_before(n - 1))
                        out = m.qp[n % 2][0:r, :].rearrange("p (h g d) -> p g h d", h=4, g=2)
                        c, y = (v[:, 0, :, :].rearrange("p (g h) d -> p g h d", g=2) for v in (c, y))
                        dve.tensor_tensor(out, c, y, ALU.add).then_inc(s["roped"], 1)
                    else:
                        dve.tensor_tensor(x, c, y, ALU.add).then_inc(s["roped"], 1)
                k = n - 1
                if here(k) and turns(k):
                    kind, t = CHUNKS[k // NT], k % NT
                    dve.wait_ge(s["tturned"], turns_before(k) + 1)
                    src = m.banks[:, 0, :]
                    if kind == "kv" and t < TP:
                        last = dve.tensor_copy(m.kselT[:, t * P:(t + 1) * P], src[:, 0:P])
                    elif kind == "kv":
                        last = dve.tensor_copy(m.ksnew, src[:, 0:NB_SEQ])
                    elif kind == "win":
                        last = dve.tensor_copy(m.kwinT[:, t * P:(t + 1) * P], src[:, 0:P])
                    elif kind == "q" and t < TP:
                        last = dve.tensor_scalar(m.qT[:, :, t * P:(t + 1) * P], src.rearrange("p (h t) -> p h t", h=4),
                                                 0.125, None, ALU.mult)
                    elif kind == "q":
                        for g in range(2):
                            last = dve.tensor_scalar(
                                m.qbd[64 * g:64 * g + 64, :, 4 * g:4 * g + 4],
                                src[64 * g:64 * g + 64, :].rearrange("p (h t) -> p t h", h=4)[:, 0:NB_SEQ, :],
                                0.125, None, ALU.mult)
                    else:
                        j = ret_before(k) % 2
                        wait(dve, "o_done", ret_before(k) - 1)
                        dve.tensor_copy(m.rT[j], src[:, 0:256].rearrange("p (a t) -> p a t", a=2))
                        last = dve.tensor_tensor(m.qd[j], src[:, 0:P], m.qdec[:, kind[1], :], ALU.mult)
                    last.then_inc(s["tkept"], 1)
                k = n - 2
                if here(k) and is_ret(k):
                    hp, j = CHUNKS[k // NT][1], ret_before(k)
                    dve.wait_ge(s["att_done"], j + 1)
                    wait(dve, "o_done", j - 1)
                    dve.tensor_tensor(m.att[j % 2], m.banks[:, 1:3, 0:P], m.dec[:, 2 * hp:2 * hp + 2, :],
                                      ALU.mult).then_inc(s["att_masked"], 1)
                k = n - 3
                if here(k) and is_ret(k):
                    hp, t, j = CHUNKS[k // NT][1], k % NT, ret_before(k)
                    dve.wait_ge(s["o_done"], j + 1)
                    dve.tensor_copy(m.oall[hp][:, t, :].rearrange("p (h d) -> p h d", h=2), m.banks[:, 3:5, 0:HD])
                    for h2 in range(2):
                        at = slice(64 * h2, 64 * h2 + 64)
                        new = m.banks[at, 5, 64 * h2:64 * h2 + 64]
                        if t == 0:
                            last = dve.tensor_copy(m.state[hp][at, :], new)
                        else:
                            last = dve.scalar_tensor_tensor(out=m.state[hp][at, :], in0=m.state[hp][at, :],
                                                            scalar=m.gchunk[at, hp:hp + 1], in1=new,
                                                            op0=ALU.mult, op1=ALU.add)
                    last.then_inc(s["state_done"], 1)

        @block.tensor
        def _(pe):
            pe.wait_ge(s["ident_in"], 16)

            def turn_half(i, half):
                r = rows(i)
                pe.wait_ge(s["h_done"], i + 1)
                wait(pe, "hT_lo", 2 * i + half)
                for k in range(4 * half, 4 * half + 4):
                    done = pe.transpose(m.banks[:, 0, P * (k % 4):P * (k % 4) + r],
                                        m.xt[i % 2][0:r, k * P:(k + 1) * P], m.ident[0:r, 0:r])
                done.then_inc(s["turned"], 1)

            if first == 0:
                turn_half(0, 0)
                turn_half(0, 1)
            for n in steps:
                if n < n1:
                    kind, ch, t = CHUNKS[n // NT], n // NT, n % NT
                    r = rows(t)
                    if n < NT:
                        pe.wait_ge(s["hT_lo"], 2 * n + 2)
                    wait(pe, "raw_done", n - 1)
                    for k in range(KT):
                        if n + 1 < NT and k in TURN_STEPS:
                            wait(pe, "tkept", turns_before(n - 1))
                            turn_half(n + 1, TURN_STEPS.index(k))
                        if t == 0:
                            pe.wait_ge(s["aw_lo"], KT * ch + k + 1)
                        last_mm = split_products(pe, m.banks[0:r, 6 + n % 2, 0:WIDTH[ch]],
                                                 [x[:, k, t * P:t * P + r] for x in m.hT],
                                                 [w[:, 0:WIDTH[ch]] for w in m.wk[k]], k == 0, k == KT - 1)
                        if t == NT - 1 and ch + 1 < end and k < KT - 1:
                            last_mm.then_inc(s["w_used"], 1)
                    last_mm.then_inc(s["proj_done"], 1)
                k = n - 1
                if here(k) and turns(k):
                    kind, t = CHUNKS[k // NT], k % NT
                    r = rows(t)
                    pe.wait_ge(s["roped"], k + 1)
                    wait(pe, "tkept", turns_before(k))
                    if n + 1 < NT:
                        pe.wait_ge(s["hT_lo"], 2 * n + 4)
                    if kind == "q":
                        src, cols = m.qp[k % 2], [0, 128, 256, 384]
                    else:
                        src, cols = m.raw[k % NRAW], [256] if kind == "kv" else [0] if kind == "win" else [0, 128]
                    for i, at in enumerate(cols):
                        last = pe.transpose(m.banks[:, 0, P * i:P * i + r], src[0:r, at:at + P], m.ident[0:r, 0:r])
                    last.then_inc(s["tturned"], 1)
                k = n - 2
                if here(k) and is_ret(k):
                    j = ret_before(k)
                    pe.wait_ge(s["tkept"], turns_before(k) + 1)
                    wait(pe, "att_masked", j)
                    for h2 in range(2):
                        at = slice(64 * h2, 64 * h2 + 64)
                        last = pe.matmul(m.banks[:, 1 + h2, 0:P], m.rT[j % 2][at, 1, :], m.rT[j % 2][at, 0, :],
                                         start=True, stop=True)
                    last.then_inc(s["att_done"], 1)
                k = n - 3
                if here(k) and is_ret(k):
                    hp, t, j = CHUNKS[k // NT][1], k % NT, ret_before(k)
                    v = m.raw[k % NRAW][:, 256:384]
                    pe.wait_ge(s["att_masked"], j + 1)
                    pe.wait_ge(s["kd_done"], j + 1)
                    wait(pe, "state_done", j)
                    for h2 in range(2):
                        at = slice(64 * h2, 64 * h2 + 64)
                        o = m.banks[:, 3 + h2, 0:HD]
                        pe.matmul(o, m.att[j % 2][:, h2, :], v[:, at], start=True, stop=(t == 0))
                        if t > 0:
                            pe.matmul(o, m.qd[j % 2][at, :], m.state[hp][at, :], start=False, stop=True)
                    pe.matmul(m.banks[:, 5, 0:P], m.kd[j % 2], v, start=True, stop=True).then_inc(s["o_done"], 1)


STEPS_B = range(NB_SEQ + 3)
SEQS_B = range(NB_SEQ + 1)


EARLY_ROWS = 14


def load_prompt_rows(sp, s, io, dst, t0, t1, done):
    sp.dma_start(dst.rearrange("p (t n) -> p t n", t=t1 - t0), io.kvp.rearrange("(c t) n -> c t n", t=CH)[:, t0:t1, 0:256]
                 ).then_inc(s[done], 16)


def chunks_of(q):
    return (SEQ if q == 0 else PAST) // CH


def turn_uses():
    uses = []
    for step in STEPS_B:
        a = step - 1
        if step in SEQS_B:
            uses += [("k", step, i) for i in range(4)]
        if 1 <= a <= NB_SEQ:
            uses += [("s", a, i) for i in range(5)]
        if step in SEQS_B:
            uses += [("v", step, i) for i in range(4)]
    return uses


TURNS = turn_uses()
TURN_AT = {u: i for i, u in enumerate(TURNS)}


def kept_by(count, dve):
    return sum((u[0] == "s") == dve for u in TURNS[:count])


def pad_queries(pool, s, m, t):
    if t >= 2:
        pool.wait_ge(s["c_scores"], 24 * (t - 1))
    for g in range(2):
        at = slice(HD * g, HD * g + HD)
        pool.tensor_copy(m.qz[t % 2][at, :, g, :], m.qT[at, :, P * t:P * t + P]).then_inc(s["c_queries"], 1)


def prepare_attention(pool, s, m):
    for b16, f32 in ((m.identb, m.ident), (m.cmpb16, m.cmp_mask), (m.causalb, m.causal), (m.edgeb, m.edge)):
        pool.tensor_copy(b16, f32).then_inc(s["c_masks"], 1)
    pool.wait_ge(s["b_turned"], TURN_AT["v", NB_SEQ, 3] + 1)
    for t in range(2):
        if t:
            pool.wait_ge(s["c_queries"], 2 * t)
        pool.memset(m.qz[t], 0.0).then_inc(s["c_zeroed"], 1)
        pool.wait_ge(s["c_zeroed"], t + 1)
        pad_queries(pool, s, m, t)
    pool.wait_ge(s["c_queries"], 4)


def stage_sequences(nc, s, m, io):
    wait = s.wait
    NPG = PAST // PAGE
    CMP, SEL, WINC = slice(0, 127), slice(127, 2176), slice(2176, 2688)
    SR = m.SR[0:8, :]
    bst = m.bst[0:8, :]

    NR = NB_SEQ * 8
    S0, S2 = m.S0[0:NR, :], m.S2[0:NR, :]
    S0v, S2v = (v.rearrange("p (d e) -> p d e", d=HD) for v in (S0, S2))
    rq, rk, rv, rg = (m.R4[0:NR, j, :] for j in range(4))
    ro, rk8, prod, qs = (m.rsm[0:NR, HD * j:HD * j + HD] for j in range(4))
    qk, ss, rms, rstd = (m.rst[0:NR, 64 + j:65 + j] for j in range(4))

    def free_turn_bank(eng, i):
        if i >= 2:
            wait(eng, "b_kept_dve", kept_by(i - 1, True))
            wait(eng, "b_kept_act", kept_by(i - 1, False))

    with nc.Block() as block:

        @block.sync
        def _(sp):
            load_prompt_rows(sp, s, io, m.pool[0:64, 256 * EARLY_ROWS:4096], EARLY_ROWS, CH, "cmp_in")
            for x, done in enumerate(("b_w_first", "b_w_in0")):
                dst, src = (w.rearrange("p (a k) n -> p a k n", a=2)[:, :, 4 * x:4 * x + 4, :] for w in (m.w1[0], io.w1[0]))
                for a in range(2):
                    sp.dma_start(dst[:, a, :, :], src[:, a, :, :]).then_inc(s[done], 16)
            sp.dma_start(m.pages[0:1, :], io.table).then_inc(s["pages_in"], 16)
            for kv in range(2):
                if kv:
                    sp.dma_start(m.w1[kv], io.w1[kv]).then_inc(s[f"b_w_in{kv}"], 16)
                sp.dma_start(m.w2[kv], io.w2[kv]).then_inc(s[f"b_w_in{kv}"], 16)
                with nc.allow_non_contiguous_dma(reason="the 32 x 64 position rows, turned"):
                    sp.dma_start(m.posT[kv], io.pos[kv]).then_inc(s[f"b_w_in{kv}"], 16)
            sp.dma_start(m.R4[0:NR, :, :], io.ret_rows.rearrange("b h j e -> (b h) j e")).then_inc(s["r_rows_in"], 16)
            sp.dma_start(m.gs[0:8, :, :], io.gate_rows.rearrange("b (r n) -> r b n", r=8)).then_inc(s["gs_in"], 16)
            sp.wait_ge(s["pages_in"], 16)

            def pages(q, dst, lo, n, done):
                for pg, page in enumerate(page_of[q]):
                    sp.dma_start(dst[8 * pg:8 * pg + 8, :, :],
                                 io.pool[bass.ds(page, 1), :, :, lo:lo + n].rearrange("a c t n -> (a c) t n")
                                 ).then_inc(s[done], 16)

            page_of = {}

            def retention_out():
                sp.wait_ge(s["r_o"], 1)
                sp.dma_start(io.ret_out.rearrange("b (h e) -> (b h) e", e=HD), ro).then_inc(s["r_o_out"], 16)
                sp.wait_ge(s["r_new_state"], 1)
                sp.dma_start(io.state_out, S0).then_inc(s["r_state_out"], 16)
                sp.wait_ge(s["r_o_out"], 16)
                sp.dma_start(m.rrow[0:NB_SEQ, :], io.ret_out).then_inc(s["r_o_in"], 16)

            for step in STEPS_B:
                if step + 1 <= NB_SEQ:
                    page_of.pop(step - 2, None)
                    at = NPG * step
                    page_of[step + 1] = [sp.value_load(m.pages[0:1, x:x + 1], min_val=0, max_val=NPOOL - 1)
                                         for x in range(at, at + NPG)]
                q = step + 1
                if q <= NB_SEQ:
                    sp.wait_ge(s["b_grouped"], 2 * q - 1)
                    if q == 1:
                        sp.wait_ge(s["b_first"], 2)
                    pages(q, m.cmpb, 0, 256, "cmp_in")
                if step == 0:
                    sp.dma_start(S0, io.state_in).then_inc(s["r_state_in"], 16)
                    sp.dma_start(m.cst, io.const[:, N_LATE:]).then_inc(s["const_in"], 16)
                elif step == 1:
                    retention_out()
                q = step - 1
                if 1 <= q <= NB_SEQ:
                    wait(sp, "pv_done", q - 1)
                    pages(q, m.selv, 384, 128, "values_in")
                    sp.dma_start(m.winv, io.wins[q - 1, :, :].rearrange("(p t) n -> p t n", t=4)[:, :, 128:256]
                                 ).then_inc(s["values_in"], 16)
                    sp.dma_start(m.vcb[q % 2][127:128, :], io.kvs[q - 1:q, 384:512]).then_inc(s["values_in"], 16)
                q = step
                if 1 <= q <= NB_SEQ:
                    if q >= 2:
                        sp.wait_ge(s["b_turned"], TURN_AT["s", q - 1, 4] + 1)
                    pages(q, m.selk, 256, 128, "keys_in")
                    sp.dma_start(m.wink, io.wins[q - 1, :, :].rearrange("(p t) n -> p t n", t=4)[:, :, 0:128]
                                 ).then_inc(s["keys_in"], 16)

        @block.gpsimd
        def _(pool):
            for q in SEQS_B:
                for kv in range(2):
                    if q == 0 and kv == 0:
                        continue
                    n = chunks_of(q)
                    pool.wait_ge(s["cmp_early"], 16)
                    pool.wait_ge(s["cmp_in"], 16 + 16 * NPG * q)
                    if q:
                        pool.wait_ge(s["b_turned"], TURN_AT["kv"[kv], q - 1, 3] + 1)
                    pool.tensor_copy(m.cmpg[0:n, kv, :, :, :],
                                     m.cmpb[0:n, :, P * kv:P * kv + P].rearrange("p t (g d) -> p g t d", g=2)
                                     ).then_inc(s["b_grouped"], 1)

            prepare_attention(pool, s, m)

        @block.tensor
        def _(pe):
            def position_bias(kv):
                pe.wait_ge(s[f"b_w_in{kv}"], 48 if kv else 64)
                for k in range(16):
                    last = pe.matmul(m.banks[0:1, 4, 0:256], m.posT[kv][:, k:k + 1], m.w1[kv][:, k, :],
                                     start=(k == 0), stop=(k == 15))
                last.then_inc(s["b_bias"], 1)
                pe.wait_ge(s["b_bias_row"], kv + 1)
                for mt in range(2):
                    last = pe.transpose(m.banks[:, 5, mt:mt + 1], m.brow[0:1, P * mt:P * mt + P], m.ident[0:1, 0:1])
                last.then_inc(s["b_bias"], 1)

            def retention():
                pe.wait_ge(s["b_imp_read"], NB_SEQ)
                for i in range(9):
                    if i >= 2:
                        pe.wait_ge(s["r_kept"], i - 1)
                    if i < 8:
                        hp, half = divmod(i, 2)
                        pe.wait_ge(s["r_gated"], hp + 1)
                        for x in range(4):
                            last = pe.transpose(m.banks[:, 6 + i % 2, P * x:P * x + P],
                                                m.oall[hp][:, 4 * half + x, :], m.ident)
                    else:
                        pe.wait_ge(s["r_o_in"], 16)
                        for x in range(4):
                            last = pe.transpose(m.banks[:, 6 + i % 2, NB_SEQ * x:NB_SEQ * x + NB_SEQ],
                                                m.rrow[0:NB_SEQ, P * x:P * x + P], m.ident[0:NB_SEQ, 0:NB_SEQ])
                    last.then_inc(s["r_turned"], 1)
                pe.wait_ge(s["r_kept"], 9)

            def compress(q, kv):
                nch = chunks_of(q)
                nb = nch - 1
                if q or kv:
                    pe.wait_ge(s["b_grouped"], 2 * q + kv)

                def turn_rows(i):
                    u = TURN_AT["kv"[kv], q, i]
                    free_turn_bank(pe, u)
                    if q == 0 and kv == 0:
                        pe.wait_ge(s["b_first"], i // 2 + 1)
                    for x in range(4):
                        t = 4 * i + 2 * (x // 2)
                        src = m.cmpg[0:nch, kv, x % 2, t:t + 2, :].rearrange("p t d -> p (t d)")
                        last = pe.transpose(m.banks[:, u % 2, P * x:P * x + nch], src, m.ident[0:nch, 0:nch])
                    last.then_inc(s["b_turned"], 1)

                turn_rows(0)
                turn_rows(1)
                if kv == 0 and q:
                    compressed(q - 1)
                done = 2 * q + kv
                if q == 0 and kv:
                    pe.wait_ge(s["b_w_in1"], 48)
                wait(pe, "b_gelu", 2 * done)
                for i in range(4):
                    if i in (1, 2):
                        turn_rows(i + 1)
                    if done == 0 and i % 2 == 0:
                        pe.wait_ge(s["b_w_in0" if i else "b_w_first"], 64 if i else 32)
                    pe.wait_ge(s["b_kept_act"], kept_by(TURN_AT["kv"[kv], q, i] + 1, False))
                    for k in (2 * i, 2 * i + 1, 8 + 2 * i, 9 + 2 * i):
                        for mt in range(2):
                            last = pe.matmul(m.banks[:, 2 + mt, 0:2 * nb], m.w1[kv][:, k, P * mt:P * mt + P],
                                             m.XT[:, k % 8, :, k // 8:k // 8 + nb], start=(k == 0), stop=(k == 15))
                    if i == 0 and kv == 1 and 1 <= q - 1:
                        if 1 <= q - 2:
                            turn_output(q - 2)
                        importance(q - 1)
                last.then_inc(s["b_hidden"], 1)
                if q == 0:
                    position_bias(kv)
                    pe.wait_ge(s["b_bias_kept"], kv + 1)

            def compressed(q):
                nb = chunks_of(q) - 1
                pe.wait_ge(s["b_gelu"], 4 * q + 4)
                wait(pe, "pv_kept", q - 2)
                wait(pe, "pt_kept", q - 2)
                for g in range(2):
                    for mt in range(2):
                        last = pe.matmul(m.banks[64 * g:64 * g + 64, 4, 0:nb], m.w2[0][:, mt, :],
                                         m.G[0][:, mt, nb * g:nb * g + nb], start=(mt == 0), stop=(mt == 1))
                last.then_inc(s["b_kc"], 1)
                for g in range(2):
                    for mt in range(2):
                        last = pe.matmul(m.banks[0:nb, 5, 64 * g:64 * g + 64], m.G[1][:, mt, nb * g:nb * g + nb],
                                         m.w2[1][:, mt, :], start=(mt == 0), stop=(mt == 1))
                last.then_inc(s["b_vc"], 1)

            def values(q):
                pe.wait_ge(s["b_scaled"], q)
                wait(pe, "b_vc_kept", q + 2 if q + 1 <= NB_SEQ else q + 1)
                for i in range(21):
                    last = pe.transpose(m.banks[:, 5, 8 * i:8 * i + 8], SR[:, P * i:P * i + P], m.ident[0:8, 0:8])
                last.then_inc(s["pt_done"], 1)
                if q + 1 <= NB_SEQ:
                    first_keys(q + 1)
                pe.wait_ge(s["pt_kept"], q)
                pe.wait_ge(s["values_in"], 16 * (NPG + 2) * q)
                for i in range(21):
                    v = m.vcb[q % 2] if i == 0 else m.selv[:, i - 1, :] if i <= CH else m.winv[:, i - 1 - CH, :]
                    last = pe.matmul(m.banks[0:8, 4, 0:128], m.PT[:, 8 * i:8 * i + 8], v, start=(i == 0), stop=(i == 20))
                last.then_inc(s["pv_done"], 1)

            def turn_output(q):
                pe.wait_ge(s["o_kept"], q)
                pe.transpose(m.banks[:, 5, 0:8], m.osm[0:8, :], m.ident[0:8, 0:8]).then_inc(s["o_turned"], 1)

            def turn_keys(q, i):
                u = TURN_AT["s", q, i]
                free_turn_bank(pe, u)
                for x in range(4):
                    src = m.selk[:, 4 * i + x, :] if i < 4 else m.wink[:, x, :]
                    last = pe.transpose(m.banks[:, u % 2, P * x:P * x + P], src, m.ident)
                last.then_inc(s["b_turned"], 1)

            def first_keys(q):
                pe.wait_ge(s["keys_in"], 16 * (NPG + 1) * q)
                turn_keys(q, 0)
                turn_keys(q, 1)

            def scores(q):
                if q == 1:
                    first_keys(q)
                for i in range(6):
                    if 1 <= i < 4:
                        turn_keys(q, i + 1)
                    if i == 0:
                        pe.wait_ge(s["b_kc_kept"], q + 1)
                        wait(pe, "b_imp_read", q - 1)
                    if i >= 1:
                        pe.wait_ge(s["b_kept_dve"], kept_by(TURN_AT["s", q, i - 1] + 1, True))
                    wait(pe, "sc_kept", 6 * (q - 1) + i - 1)
                    rhs = m.kcb[q % 2] if i == 0 else m.kselb[:, 512 * i - 512:512 * i] if i < 5 else m.kwb
                    n = 128 if i == 0 else 512
                    pe.matmul(m.banks[0:8, 6 + i % 2, 0:n], m.qbd[:, q - 1, :], rhs, start=True, stop=True
                              ).then_inc(s["sc_done"], 1)

            def importance(q):
                pe.wait_ge(s["b_pc"], q)
                pe.wait_ge(s["sc_kept"], 6 * q)
                pe.matmul(m.banks[0:8, 6, 0:127], m.group[0:8, :], m.pcn[0:8, 0:127], start=True, stop=True
                          ).then_inc(s["b_imp"], 1)

            for step in STEPS_B:
                if step in SEQS_B:
                    compress(step, 0)
                if step == NB_SEQ + 2:
                    retention()
                if 1 <= step - 2 <= NB_SEQ:
                    values(step - 2)
                if 1 <= step - 1 <= NB_SEQ:
                    scores(step - 1)
                if step in SEQS_B:
                    compress(step, 1)
                else:
                    turn_output(step - 2)
                    if step - 1 == NB_SEQ:
                        importance(step - 1)
                if step == NB_SEQ:
                    compressed(step)

        @block.scalar
        def _(act):
            n = chunks_of(0)
            act.wait_ge(s["cmp_early"], 16)
            for half in range(2):
                if half:
                    act.wait_ge(s["cmp_in"], 16)
                act.activation(m.cmpg[0:n, 0, :, 8 * half:8 * half + 8, :],
                               m.cmpb[0:n, 8 * half:8 * half + 8, 0:P].rearrange("p t (g d) -> p g t d", g=2),
                               ACT.Copy).then_inc(s["b_first"], 1)
            def keep_bias(kv):
                act.wait_ge(s["b_bias"], 2 * kv + 1)
                act.activation(m.brow[0:1, :], m.banks[0:1, 4, 0:256], ACT.Copy).then_inc(s["b_bias_row"], 1)
                act.wait_ge(s["b_bias"], 2 * kv + 2)
                act.activation(m.cbias.rearrange("p (m k) -> p m k", m=2)[:, :, kv], m.banks[:, 5, 0:2], ACT.Copy
                               ).then_inc(s["b_bias_kept"], 1)
                act.wait_ge(s["b_bias_kept"], kv + 1)

            def keep_retention():
                for i in range(9):
                    act.wait_ge(s["r_turned"], i + 1)
                    b = m.banks[:, 6 + i % 2, :]
                    if i < 8:
                        out = m.mixT[:, 4 + i // 2, 512 * (i % 2):512 * (i % 2) + 512]
                    else:
                        out, b = m.mixT[:, 4:8, SEQ:TOK], b[:, 0:32].rearrange("p (k t) -> p k t", k=4)
                    act.activation(out, b, ACT.Copy).then_inc(s["r_kept"], 1)

            def keep_turned(q, kv, parts=range(4)):
                nch = chunks_of(q)
                if 2 * q + kv:
                    act.wait_ge(s["b_hidden"], 2 * q + kv)
                for i in parts:
                    u = TURN_AT["kv"[kv], q, i]
                    act.wait_ge(s["b_turned"], u + 1)
                    act.activation(m.XT[:, 2 * i:2 * i + 2, :, 0:nch],
                                   m.banks[:, u % 2, :].rearrange("p (j g c) -> p j g c", j=2, g=2)[:, :, :, 0:nch],
                                   ACT.Copy).then_inc(s["b_kept_act"], 1)

            def gelu(q, kv):
                nb = chunks_of(q) - 1
                act.wait_ge(s["b_hidden"], 2 * q + kv + 1)
                wait(act, "b_vc", q)
                for mt in range(2):
                    act.activation(m.G[kv][:, mt, 0:2 * nb], m.banks[:, 2 + mt, 0:2 * nb], ACT.Gelu_apprx_tanh,
                                   bias=m.cbias[:, 2 * mt + kv:2 * mt + kv + 1]).then_inc(s["b_gelu"], 1)

            keep_turned(0, 0)
            for hp in range(4):
                act.wait_ge(s["r_sums"], hp + 1)
                act.activation(m.rst[:, 16 * hp:16 * hp + 16], m.rst[:, 16 * hp:16 * hp + 16], ACT.Sqrt,
                               bias=m.small[:, 64:65], scale=1.0 / HD).then_inc(s["r_rms"], 1)
            for step in STEPS_B:
                q = step - 2
                if 1 <= q <= NB_SEQ:
                    act.wait_ge(s["b_win_max"], q)
                    act.activation(SR[:, WINC], SR[:, WINC], ACT.Exp, bias=bst[:, 3:4],
                                   accum_out=bst[:, 4:5]).then_inc(s["b_win_exp"], 1)
                    if step == NB_SEQ + 2:
                        keep_retention()
                    act.wait_ge(s["b_sel_max"], q)
                    act.activation(SR[:, SEL], SR[:, SEL], ACT.Exp, bias=bst[:, 5:6],
                                   accum_out=bst[:, 6:7]).then_inc(s["b_sel_exp"], 1)
                if step == 0:
                    keep_bias(0)
                if step in SEQS_B:
                    gelu(step, 0)
                if step == 2:
                    act.wait_ge(s["r_state_out"], 16)
                q = step - 1
                if 1 <= q <= NB_SEQ:
                    wait(act, "pt_done", q - 1)
                    for i in range(6):
                        act.wait_ge(s["sc_done"], 6 * (q - 1) + i + 1)
                        at, n = (0, 128) if i == 0 else (128 + 512 * (i - 1), 512)
                        act.activation(SR[:, at:at + n], m.banks[0:8, 6 + i % 2, 0:n], ACT.Copy
                                       ).then_inc(s["sc_kept"], 1)
                    if step in SEQS_B:
                        keep_turned(step, 1, range(2))
                    act.wait_ge(s["b_cmp_max"], q)
                    act.activation(SR[:, CMP], SR[:, CMP], ACT.Exp, bias=bst[:, 0:1],
                                   accum_out=bst[:, 1:2]).then_inc(s["b_cmp_exp"], 1)
                q = step
                if q in SEQS_B:
                    nb = chunks_of(q) - 1
                    keep_turned(q, 1, range(2 if 1 <= q - 1 <= NB_SEQ else 0, 4))
                    if q == 0:
                        keep_bias(1)
                    gelu(q, 1)
                    if q + 1 in SEQS_B:
                        keep_turned(q + 1, 0)
                    if q == 0:
                        act.wait_ge(s["r_ssum"], 1)
                        act.activation(rms, ss, ACT.Sqrt, bias=m.small[0:NR, 64:65], scale=1.0 / HD
                                       ).then_inc(s["r_srms"], 1)
                    kc, vc = (m.kcbP, m.vcbP) if q == 0 else (m.kcb[q % 2], m.vcb[q % 2])
                    act.wait_ge(s["b_kc"], q + 1)
                    if q:
                        act.activation(kc[:, 127:128], m.ksnew[:, q - 1:q], ACT.Copy)
                    act.activation(kc[:, 0:nb], m.banks[:, 4, 0:nb], ACT.Copy).then_inc(s["b_kc_kept"], 1)
                    act.wait_ge(s["b_vc"], q + 1)
                    wait(act, "pv_done", q - 2)
                    act.activation(vc[0:nb, :], m.banks[0:nb, 5, 0:128], ACT.Copy).then_inc(s["b_vc_kept"], 1)

        @block.vector
        def _(dve):
            own = Links(dve, s, "own_dve")
            own.after(dve.memset(m.blkm[0:8, :], 0.0))
            for hp in range(4):
                o, sums = m.oall[hp], m.rst[:, 16 * hp:16 * hp + 16]
                own.after(dve.tensor_tensor(m.rsq.rearrange("p (t n) -> p t n", t=TP), o, o, ALU.mult))
                dve.tensor_reduce(sums, m.rsq.rearrange("p (t d) -> p t d", d=HD), AX.X, ALU.add
                                  ).then_inc(s["r_sums"], 1)
                dve.wait_ge(s["r_sums"], hp + 1)
            for hp in range(4):
                heads_o, sums = m.oall[hp].rearrange("p t (h d) -> p (t h) d", h=2), m.rst[:, 16 * hp:16 * hp + 16]
                dve.wait_ge(s["r_rms"], hp + 1)
                own.after(dve.reciprocal(sums, sums))
                own.after(dve.tensor_tensor(heads_o, heads_o, sums.unsqueeze(2).broadcast_to(heads_o.shape), ALU.mult))
                dve.tensor_tensor(m.oall[hp], m.oall[hp], m.gall[hp], ALU.mult).then_inc(s["r_gated"], 1)
            dve.wait_ge(s["r_gated"], 4)
            dve.wait_ge(s["const_in"], 48)
            dve.wait_ge(s["r_rows_in"], 16)
            own.after(dve.tensor_scalar(rk8, rk, 0.125, None, ALU.mult))
            own.after(dve.tensor_tensor(prod, rq, rk8, ALU.mult))
            own.after(dve.tensor_reduce(qk, prod, AX.X, ALU.add))
            own.after(dve.tensor_scalar(ro, rv, qk, None, ALU.mult))
            dve.wait_ge(s["r_state_in"], 16)
            own.after(dve.tensor_tensor(S2v, S0v.rearrange("p d e -> p e d"), rq.unsqueeze(1).broadcast_to(S2v.shape),
                                        ALU.mult))
            own.after(dve.tensor_reduce(qs, S2v, AX.X, ALU.add))
            own.after(dve.scalar_tensor_tensor(out=ro, in0=qs, scalar=m.gone[0:NR, :], in1=ro, op0=ALU.mult,
                                               op1=ALU.add))
            own.after(dve.tensor_tensor(prod, ro, ro, ALU.mult))
            dve.tensor_reduce(ss, prod, AX.X, ALU.add).then_inc(s["r_ssum"], 1)
            own.after(dve.tensor_tensor(S2v, rk8.unsqueeze(2).broadcast_to(S2v.shape),
                                        rv.unsqueeze(1).broadcast_to(S2v.shape), ALU.mult))
            dve.wait_ge(s["r_srms"], 1)
            own.after(dve.reciprocal(rstd, rms))
            dve.scalar_tensor_tensor(out=ro, in0=ro, scalar=rstd, in1=rg, op0=ALU.mult, op1=ALU.mult).then_inc(s["r_o"], 1)
            dve.scalar_tensor_tensor(out=S0, in0=S0, scalar=m.gone[0:NR, :], in1=S2, op0=ALU.mult,
                                     op1=ALU.add).then_inc(s["r_new_state"], 1)
            dve.wait_ge(s["r_new_state"], 1)
            dve.wait_ge(s["r_state_out"], 16)
            dve.wait_ge(s["gs_in"], 16)

            def inverse(total, gate, out):
                own.after(dve.tensor_scalar(total, total, 1e-30, None, ALU.max))
                own.after(dve.reciprocal(total, total))
                if gate is not None:
                    own.after(dve.tensor_tensor(out, total, gate, ALU.mult))

            def keep_keys(q, parts):
                wait(dve, "sc_done", 6 * (q - 1))
                for i in parts:
                    u = TURN_AT["s", q, i]
                    dve.wait_ge(s["b_turned"], u + 1)
                    dst = m.kselb[:, 512 * i:512 * i + 512] if i < 4 else m.kwb
                    dve.tensor_copy(dst, m.banks[:, u % 2, :]).then_inc(s["b_kept_dve"], 1)

            def keep_output(q):
                dve.wait_ge(s["o_turned"], q)
                for g in range(2):
                    at = slice(64 * g, 64 * g + 64)
                    last = dve.tensor_copy(m.mixT[at, 0:4, SEQ + q - 1:SEQ + q].rearrange("p h t -> p (h t)"),
                                           m.banks[at, 5, 4 * g:4 * g + 4])
                last.then_inc(s["pv_kept"], 1)

            for step in STEPS_B:
                q = step - 2
                if 1 <= q <= NB_SEQ:
                    dve.wait_ge(s["b_win_exp"], q)
                    inverse(bst[:, 4:5], m.gs[0:8, q - 1, 2:3], bst[:, 7:8])
                    dve.tensor_scalar(SR[:, WINC], SR[:, WINC], bst[:, 7:8], None, ALU.mult)
                    dve.wait_ge(s["b_sel_exp"], q)
                    inverse(bst[:, 6:7], m.gs[0:8, q - 1, 1:2], bst[:, 8:9])
                    dve.tensor_scalar(SR[:, SEL], SR[:, SEL], bst[:, 8:9], None, ALU.mult).then_inc(s["b_scaled"], 1)
                    dve.wait_ge(s["pt_done"], q)
                    wait(dve, "pv_done", q - 1)
                    dve.tensor_copy(m.PT, m.banks[:, 5, 0:168]).then_inc(s["pt_kept"], 1)
                    if q + 1 <= NB_SEQ:
                        keep_keys(q + 1, range(2))
                    dve.wait_ge(s["pv_done"], q)
                    dve.tensor_copy(m.osm[0:8, :], m.banks[0:8, 4, 0:128]).then_inc(s["o_kept"], 1)
                    if step - 1 > NB_SEQ:
                        keep_output(q)
                q = step - 1
                if 1 <= q <= NB_SEQ:
                    keep_keys(q, range(0 if q == 1 else 2, 5))
                    dve.wait_ge(s["sc_kept"], 6 * (q - 1) + 1)
                    dve.tensor_reduce(bst[:, 0:1], SR[:, CMP], AX.X, ALU.max, negate=True).then_inc(s["b_cmp_max"], 1)
                    dve.wait_ge(s["sc_kept"], 6 * q)
                    dve.tensor_reduce(bst[:, 3:4], SR[:, WINC], AX.X, ALU.max, negate=True).then_inc(s["b_win_max"], 1)
                    dve.wait_ge(s["b_cmp_exp"], q)
                    inverse(bst[:, 1:2], None, None)
                    dve.tensor_scalar(m.pcn[0:8, 0:127], SR[:, CMP], bst[:, 1:2], None, ALU.mult).then_inc(s["b_pc"], 1)
                    dve.wait_ge(s["b_pc"], q)
                    own.after(dve.tensor_scalar(SR[:, CMP], m.pcn[0:8, 0:127], m.gs[0:8, q - 1, 0:1], None, ALU.mult))
                    if q >= 2:
                        keep_output(q - 1)
                    dve.wait_ge(s["b_imp"], q)
                    imp, by = m.imp[0:8, 0:NRANK], m.banks[0:8, 6, :]
                    own.after(dve.tensor_reduce(imp, by[:, 4:124].rearrange("p (j n) -> p j n", n=4), AX.X, ALU.add))
                    dve.tensor_tensor(imp, by[:, 0:120].rearrange("p (j n) -> p j n", n=4)[:, :, 3], imp, ALU.add
                                      ).then_inc(s["b_imp_read"], 1)
                    dve.wait_ge(s["b_imp_read"], q)
                    other = imp.unsqueeze(1).broadcast_to((8, NRANK, NRANK))
                    mine = imp.unsqueeze(2).broadcast_to((8, NRANK, NRANK))
                    cg, ce = m.cg[0:8], m.ce[0:8]
                    dve.tensor_tensor(cg, other, mine, ALU.is_gt)
                    own.after(dve.tensor_tensor(ce, other, mine, ALU.is_equal))
                    own.after(dve.tensor_tensor(ce, ce, m.tie[0:8], ALU.mult))
                    own.after(dve.tensor_tensor(cg, cg, ce, ALU.add))
                    own.after(dve.tensor_reduce(imp, cg, AX.X, ALU.add))
                    own.after(dve.tensor_scalar(m.blkm[0:8, 1:1 + NRANK], imp, TOP - 0.5, NEG, ALU.is_gt, ALU.mult))
                    keys = SR[:, 128:2176].rearrange("p (t b c) -> p t b c", t=CH, c=4)
                    own.after(dve.tensor_tensor(keys, keys,
                                                m.blkm[0:8, :].unsqueeze(1).unsqueeze(3).broadcast_to(keys.shape), ALU.add))
                    dve.tensor_reduce(bst[:, 5:6], SR[:, SEL], AX.X, ALU.max, negate=True).then_inc(s["b_sel_max"], 1)


UNITS = [(t, hh, g, br) for t in range(TP) for hh in range(4) for g in range(2) for br in range(3)]
PER_TILE = 24
AHEAD = 3
BANK_C = [4, 0, 2]
OBLK = 8


def key_tiles(u):
    t, _, _, br = UNITS[u]
    return 1 if br == 0 else t + 1 if br == 1 else min(t, 4) + 1


def attention_events():
    turn, events = [], [("S", u) for u in range(AHEAD)]

    def add(what):
        turn.append(what)
        events.append(("T", len(turn) - 1))

    def values(upto):
        while done[0] < upto:
            i = done[0]
            if turn[i][0] != "mix":
                u, first, n = turn[i]
                if u % OBLK == 0 and u and first == 0 and i == upto - 1 and not last_call:
                    return
                events.append(("V", i))
                if u % PER_TILE == PER_TILE - 1 and first + n == key_tiles(u):
                    events.append(("E", UNITS[u][0]))
            done[0] += 1

    done, last_call = [0], []
    for u in range(len(UNITS)):
        for first in range(0, key_tiles(u), 4):
            add((u, first, min(4, key_tiles(u) - first)))
            if first == 0 and u + AHEAD < len(UNITS):
                events.append(("S", u + AHEAD))
            values(len(turn) - 1)
        if u % PER_TILE == 3 and u > PER_TILE:
            events.append(("F", UNITS[u][0] - 1))
        if u % PER_TILE == 6 and u > PER_TILE:
            add(("mix", UNITS[u][0] - 1))
            values(len(turn) - 1)
    last_call.append(True)
    values(len(turn))
    events.append(("F", TP - 1))
    turn.append(("mix", TP - 1))
    events.append(("T", len(turn) - 1))
    return turn, events


TURNS_C, EVENTS_C = attention_events()


def on_dve(i):
    return TURNS_C[i][0] != "mix" and i % 2 == 0


def copied_before(i, dve):
    return sum(on_dve(k) == dve for k in range(i))


def values_before(i):
    return sum(TURNS_C[k][0] != "mix" for k in range(i))


def load_w_out(sp, s, m, io, k):
    slot, name = m.slot[k % NSLOT], f"wo_in{k % NSLOT}"
    if k < 4:
        for g in range(2):
            at = 256 * g + HD * k
            sp.dma_start(slot[HD * g:HD * g + HD, :], io.w_out[at:at + HD, :]).then_inc(s[name], 16)
    else:
        sp.dma_start(slot, io.w_out[P * k:P * k + P, :]).then_inc(s[name], 16)


def stage_attention(nc, s, m, io):
    wait = s.wait

    def scores_of(u, n):
        b = BANK_C[UNITS[u][3]]
        return m.banks[:, b:min(b + 2, 5), :].rearrange("p a n -> p (a n)")[:, 0:n]

    def width(u):
        return 63 if UNITS[u][3] == 0 else P * key_tiles(u)

    def pieces(u):
        t, _, _, br = UNITS[u]
        n = width(u)
        if br == 0:
            return [(0, n, "cmp")]
        edge = [(0, P, "edge")] if br == 2 and t >= 4 else []
        lo = P * len(edge)
        return edge + [(x, min(512 * (x // 512 + 1), n - P), None) for x in ([lo] if lo < n - P else []) +
                       [y for y in (512,) if lo < y < n - P]] + [(n - P, n, "causal")]

    def ends_block(i):
        u, first, n = TURNS_C[i]
        return u % OBLK == OBLK - 1 and first + n == key_tiles(u)

    with nc.Block() as block:

        @block.sync
        def _(sp):
            for k in range(NSLOT):
                load_w_out(sp, s, m, io, k)
            sp.dma_start(m.lnb, io.ln2[0:1, :].to_broadcast((P, DM))).then_inc(s["ln2_in"], 16)

        @block.tensor
        def _(pe):
            pe.wait_ge(s["c_masks"], 4)
            for what, i in EVENTS_C:
                if what == "S":
                    t, hh, g, br = UNITS[i]
                    pe.wait_ge(s["c_queries"], 2 * t + 2)
                    wait(pe, "c_exp", i - 2)
                    first = P * (t + 1) - width(i)
                    keys = m.kcbP if br == 0 else m.kselT if br == 1 else m.kwinT[:, first:first + width(i)]
                    out = scores_of(i, width(i))
                    for lo, hi, mask in pieces(i):
                        last = pe.matmul(out[:, lo:hi], m.qz[t % 2][:, hh, g, :], keys[:, lo:hi], start=True, stop=not mask)
                        if mask:
                            add = {"cmp": m.cmpb16[:, t, :], "causal": m.causalb, "edge": m.edgeb}[mask]
                            last = pe.matmul(out[:, lo:hi], m.identb, add, start=False, stop=True)
                    last.then_inc(s["c_scores"], 1)
                elif what == "T":
                    wait(pe, "c_kept_dve", copied_before(i - 1, True))
                    wait(pe, "c_kept_act", copied_before(i - 1, False))
                    if TURNS_C[i][0] == "mix":
                        pe.wait_ge(s["c_osum"], TURNS_C[i][1] + 1)
                        for x in range(4):
                            last = pe.transpose(m.banks[:, 5 + i % 2, P * x:P * x + P], m.osum[:, P * x:P * x + P], m.ident)
                    else:
                        u, first, n = TURNS_C[i]
                        w = min(P, width(u))
                        pe.wait_ge(s["c_exp"], u + 1)
                        for x in range(n):
                            last = pe.transpose(m.banks[0:w, 5 + i % 2, P * x:P * x + P],
                                                m.prob[u % 4][:, P * (first + x):P * (first + x) + w], m.ident)
                    last.then_inc(s["c_turned"], 1)
                elif what == "V":
                    u, first, n = TURNS_C[i]
                    t, hh, g, br = UNITS[u]
                    w = min(P, width(u))
                    wait(pe, "c_okept", u // OBLK)
                    wait(pe, "c_kept_dve" if on_dve(i) else "c_kept_act", copied_before(i + 1, on_dve(i)))
                    for x in range(n):
                        k = first + x + (t + 1 - key_tiles(u) if br == 2 else 0)
                        v = m.vcbP if br == 0 else m.vsel[:, k, :] if br == 1 else m.vwin[:, k, :]
                        last = pe.matmul(m.banks[:, 7, HD * (u % 8):HD * (u % 8) + HD],
                                         m.pts[i % 3][0:w, P * x:P * x + P], v[0:w, 64 * g:64 * g + 64],
                                         start=(first + x == 0), stop=(first + x == key_tiles(u) - 1))
                    last.then_inc(s["c_pv"], 1)

        @block.scalar
        def _(act):
            order = list(EVENTS_C)
            for x, (what, i) in enumerate(EVENTS_C):
                if what == "V" and ends_block(i) and order[x - 1][0] == "S":
                    order[x - 1], order[x] = order[x], order[x - 1]
            for what, i in order:
                if what == "S":
                    act.wait_ge(s["c_max"], i + 1)
                    if i >= 4:
                        act.wait_ge(s["c_turned"], 1 + max(k for k, x in enumerate(TURNS_C) if x[0] == i - 4))
                    wait(act, "c_inverted", UNITS[i][0] - 1)
                    act.activation(m.prob[i % 4][:, 0:width(i)], scores_of(i, width(i)), ACT.Exp,
                                   bias=m.nmax[:, i % 8:i % 8 + 1],
                                   accum_out=m.sums[UNITS[i][0] % 2][:, i % PER_TILE:i % PER_TILE + 1]
                                   ).then_inc(s["c_exp"], 1)
                elif what == "T" and not on_dve(i):
                    act.wait_ge(s["c_turned"], i + 1)
                    if TURNS_C[i][0] == "mix":
                        t = TURNS_C[i][1]
                        act.activation(m.mixT[:, 0:4, P * t:P * t + P],
                                       m.banks[:, 5 + i % 2, :].rearrange("p (h t) -> p h t", h=4), ACT.Copy
                                       ).then_inc(s["c_kept_act"], 1)
                    else:
                        u, first, n = TURNS_C[i]
                        w = min(P, width(u))
                        wait(act, "c_pv", values_before(i - 2))
                        act.activation(m.pts[i % 3][0:w, 0:P * n], m.banks[0:w, 5 + i % 2, 0:P * n], ACT.Copy
                                       ).then_inc(s["c_kept_act"], 1)
                elif what == "V" and ends_block(i):
                    b, per = TURNS_C[i][0] // OBLK, PER_TILE // OBLK
                    act.wait_ge(s["c_pv"], values_before(i + 1))
                    wait(act, "c_osum", b // per - 1)
                    act.activation(m.oraw[b // per % 2][:, OBLK * (b % per):OBLK * (b % per) + OBLK, :],
                                   m.banks[:, 7, :].rearrange("p (u d) -> p u d", u=OBLK),
                                   ACT.Copy).then_inc(s["c_okept"], 1)

        @block.gpsimd
        def _(pool):
            for t in range(TP):
                if t + 2 < TP:
                    pad_queries(pool, s, m, t + 2)
                if t == TP - 1:
                    break
                pool.wait_ge(s["c_queries"], 2 * min(t + 3, TP))
                pool.wait_ge(s["c_inverted"], t + 1)
                pool.wait_ge(s["c_okept"], PER_TILE // OBLK * (t + 1))
                pool.tensor_tensor(m.oraw[t % 2], m.oraw[t % 2], m.rsc.unsqueeze(2).broadcast_to((P, PER_TILE, HD)), ALU.mult
                                   ).then_inc(s["c_weighted"], 1)

        @block.vector
        def _(dve):
            own = Links(dve, s, "own_dve")
            for what, i in EVENTS_C:
                if what == "S":
                    t, hh, g, br = UNITS[i]
                    n = width(i)
                    out = scores_of(i, n)
                    dve.wait_ge(s["c_scores"], i + 1)
                    peak = m.nmax[:, i % 8:i % 8 + 1]
                    wait(dve, "c_exp", i - 7)
                    if br == 0 and t == 0:
                        own.after(dve.tensor_reduce(peak, out, AX.X, ALU.max, negate=True))
                        dve.tensor_scalar(peak, peak, -0.1 * NEG, None, ALU.min).then_inc(s["c_max"], 1)
                    else:
                        dve.tensor_reduce(peak, out, AX.X, ALU.max, negate=True).then_inc(s["c_max"], 1)
                elif what == "T" and on_dve(i):
                    u, first, n = TURNS_C[i]
                    w = min(P, width(u))
                    dve.wait_ge(s["c_turned"], i + 1)
                    wait(dve, "c_pv", values_before(i - 2))
                    dve.tensor_copy(m.pts[i % 3][0:w, 0:P * n], m.banks[0:w, 5 + i % 2, 0:P * n]
                                    ).then_inc(s["c_kept_dve"], 1)
                elif what == "E":
                    t, sums = i, m.sums[i % 2]
                    dve.wait_ge(s["c_exp"], PER_TILE * (t + 1))
                    wait(dve, "c_weighted", t)
                    own.after(dve.tensor_scalar(sums, sums, 1e-30, None, ALU.max))
                    own.after(dve.reciprocal(m.rsc, sums))
                    dve.tensor_tensor(m.rsc.rearrange("p (h g r) -> p h g r", h=4, g=2),
                                      m.rsc.rearrange("p (h g r) -> p h g r", h=4, g=2),
                                      m.gates[:, t, :].rearrange("p (g h r) -> p h g r", g=2, h=4), ALU.mult
                                      ).then_inc(s["c_inverted"], 1)
                elif what == "F":
                    t = i
                    if t < TP - 1:
                        dve.wait_ge(s["c_weighted"], t + 1)
                    else:
                        dve.wait_ge(s["c_inverted"], TP)
                        dve.wait_ge(s["c_okept"], PER_TILE // OBLK * TP)
                        own.after(dve.tensor_tensor(m.oraw[t % 2], m.oraw[t % 2],
                                                    m.rsc.unsqueeze(2).broadcast_to((P, PER_TILE, HD)), ALU.mult))
                    if t:
                        dve.wait_ge(s["c_turned"], 1 + [x[0:2] for x in TURNS_C].index(("mix", t - 1)))
                    dve.tensor_reduce(m.osum.rearrange("p (a d) -> p a d", d=HD),
                                      m.oraw[t % 2].rearrange("p (a r) d -> p a d r", r=3), AX.X, ALU.add
                                      ).then_inc(s["c_osum"], 1)


def load_ffn_weights(sp, s, m, io, phase, g, r, first=0):
    part, what = divmod(phase, 2)
    f0, nf = PARTS[part]
    if what == 0:
        w = (io.w_gate, io.w_up)[r]
        sp.dma_start(m.wstage[r].rearrange("p (k n) -> p k n", k=KT), w[:, :, bass.ds((g + f0) * P, P)]
                     ).then_inc(s[f"ffw_in{r}"], 16)
    else:
        sp.dma_start(m.wstage[r][:, 0:nf * P].rearrange("p (k n) -> p k n", k=nf),
                     io.w_down[:, f0:f0 + nf, bass.ds((g * 2 + r) * P, P)]).then_inc(s[f"ffw_in{r}"], 16)


def stage_mix_out(nc, s, m, io):
    wait = s.wait
    with nc.Block() as block:

        @block.sync
        def _(sp):
            for k in range(NSLOT, 8):
                sp.wait_ge(s["wo_lo"], k - NSLOT + 1)
                load_w_out(sp, s, m, io, k)
            for i in range(NT + 1):
                if i < NT:
                    if i < 2:
                        sp.wait_ge(s["wo_lo"], 3 + i)
                    else:
                        sp.wait_ge(s[f"mid_out{i % 2}"], 16 * (i // 2))
                        sp.wait_ge(s["d_h"], i - 1)
                    src = io.xp[i * P:(i + 1) * P, :] if i < TP else io.xs
                    sp.dma_start(m.xr[i % 2][0:rows(i), :], src).then_inc(s[f"d_x{i % 2}"], 16)
                if i == 1:
                    sp.wait_ge(s["wo_lo"], 8)
                    for r in range(2):
                        load_ffn_weights(sp, s, m, io, 0, 0, r)
                if i >= 1:
                    k = i - 1
                    sp.wait_ge(s["d_mid"], k + 1)
                    sp.dma_start(io.mid[k * P:k * P + rows(k), :], m.xr[k % 2][0:rows(k), :]
                                 ).then_inc(s[f"mid_out{k % 2}"], 16)
            sp.wait_ge(s["mid_out0"], 16 * 5)
            sp.wait_ge(s["mid_out1"], 16 * 4)

        @block.tensor
        def _(pe):
            for i in range(NT + 1):
                if i < NT:
                    r = rows(i)
                    pe.wait_ge(s["mix_lo"], i + 1)
                    wait(pe, "d_mid", i - 1)
                    for k in range(8):
                        if i == 0:
                            pe.wait_ge(s["wo_lo"], k + 1)
                        for n in range(2):
                            last = split_products(pe, m.banks[0:r, 2 * (i % 2) + n, :],
                                                  [x[:, k, 0:r] for x in m.mix[i % 2]],
                                                  [x[:, k, 512 * n:512 * n + 512] for x in m.wo], k == 0, k == 7)
                    last.then_inc(s["d_mm"], 1)
                if i >= 1:
                    j = i - 1
                    r = rows(j)
                    pe.wait_ge(s["d_h"], j + 1)
                    wait(pe, "h2_lo", j - 1)
                    for k in range(KT):
                        last = pe.transpose(m.banks[:, 4 + 2 * (j % 2) + k // 4, P * (k % 4):P * (k % 4) + r],
                                            m.dh[j % 2][0:r, P * k:P * k + P], m.ident[0:r, 0:r])
                    last.then_inc(s["d_turned"], 1)

        def tile_of(v, i):
            return v[:, :, i * P:i * P + rows(i)]

        def turned(j, half):
            b = m.banks[:, 4 + 2 * (j % 2) + half, :].rearrange("p (k t) -> p k t", k=4)[:, :, 0:rows(j)]
            return b, [tile_of(v, j)[:, 4 * half:4 * half + 4, :] for v in m.h2T]

        @block.scalar
        def _(act):
            own = Links(act, s, "own_act")

            def mix_hi(i):
                wait(act, "d_mm", i - 1)
                round_to_hi(act, m.mix[i % 2][0][:, :, 0:rows(i)], tile_of(m.mixT, i)).then_inc(s["mix_hi"], 1)

            for k in range(8):
                act.wait_ge(s[f"wo_in{k % NSLOT}"], 16 * (2 if k < 4 else 1) + (32 if k >= NSLOT else 0))
                round_to_hi(act, m.wo[0][:, k, :], m.slot[k % NSLOT]).then_inc(s["wo_hi"], 1)
                if k == 0:
                    mix_hi(0)
            act.wait_ge(s["wo_lo"], 6)
            for i in range(NT + 1):
                if i + 1 < NT:
                    mix_hi(i + 1)
                if i < NT:
                    r = rows(i)
                    act.wait_ge(s["d_mid"], i + 1)
                    wait(act, "d_turned", i - 1)
                    own.after(act.activation(m.dh[i % 2][0:r, :], m.xr[i % 2][0:r, :], ACT.Square,
                                             accum_out=m.small[0:r, i:i + 1]))
                    act.activation(m.small[0:r, 16 + i:17 + i], m.small[0:r, i:i + 1], ACT.Sqrt,
                                   bias=m.small[0:r, 64:65], scale=1.0 / DM).then_inc(s["d_rms"], 1)
                if i >= 1:
                    act.wait_ge(s["d_turned"], i)
                    for half in range(2):
                        b, (hi, _) = turned(i - 1, half)
                        round_to_hi(act, hi, b).then_inc(s["h2_hi"], 1)

        @block.gpsimd
        def _(pool):
            for i in range(NT):
                pool.wait_ge(s["mix_hi"], i + 1)
                rest_to_lo(pool, m.mix[i % 2][1][:, :, 0:rows(i)], tile_of(m.mixT, i), m.mix[i % 2][0][:, :, 0:rows(i)]
                           ).then_inc(s["mix_lo"], 1)

        @block.vector
        def _(dve):
            own = Links(dve, s, "own_dve")
            for k in range(8):
                dve.wait_ge(s["wo_hi"], k + 1)
                rest_to_lo(dve, m.wo[1][:, k, :], m.slot[k % NSLOT], m.wo[0][:, k, :]).then_inc(s["wo_lo"], 1)
            dve.wait_ge(s["ln2_in"], 16)
            for i in range(NT + 1):
                if i < NT:
                    r = rows(i)
                    x = m.xr[i % 2][0:r, :]
                    dve.wait_ge(s[f"d_x{i % 2}"], 16 * (i // 2 + 1))
                    dve.wait_ge(s["d_mm"], i + 1)
                    b = m.banks[0:r, 2 * (i % 2):2 * (i % 2) + 2, :].rearrange("p a n -> p (a n)")
                    dve.tensor_tensor(x, b, x, ALU.add).then_inc(s["d_mid"], 1)
                    dve.wait_ge(s["d_rms"], i + 1)
                    own.after(dve.reciprocal(m.small[0:r, 32 + i:33 + i], m.small[0:r, 16 + i:17 + i]))
                    dve.scalar_tensor_tensor(out=m.dh[i % 2][0:r, :], in0=x, scalar=m.small[0:r, 32 + i:33 + i],
                                             in1=m.lnb[0:r, :], op0=ALU.mult, op1=ALU.mult).then_inc(s["d_h"], 1)
                if i >= 1:
                    for half in range(2):
                        b, (hi, lo) = turned(i - 1, half)
                        dve.wait_ge(s["h2_hi"], 2 * (i - 1) + half + 1)
                        last = rest_to_lo(dve, lo, b, hi)
                    last.then_inc(s["h2_lo"], 1)


PAIRS = [n for _, nf in PARTS for n in (nf, KT // 2)][:-1]
PAIR0 = [sum(PAIRS[:i]) for i in range(len(PAIRS) + 1)]
NE = sum(nf for _, nf in PARTS)
GROUPS = [(0, 4), (4, 6), (6, NT)]


def stage_feed_forward(nc, s, m, io):
    wait = s.wait
    tok = [slice(TC * q, TC * q + TC) for q in range(3)]
    ROUNDS = PAIR0[-1]
    ph_pairs = [(i, PAIRS[i], PAIR0[i], i % 2 == 0, sum(PAIRS[0:i:2])) for i in range(len(PAIRS))]
    group_tok = [(a * P, min(b * P, TOK)) for a, b in GROUPS]

    def last_order(products, tile):
        for j in range(len(GROUPS) + 1):
            tiles = list(range(*GROUPS[j - 1])) if j else []
            for n in range(KT):
                if j < len(GROUPS):
                    products(j, n)
                if n % 2 and tiles:
                    tile(tiles.pop(0))
            assert not tiles

    with nc.Block() as block:

        @block.sync
        def _(sp):
            sp.dma_start(m.lnb, io.ln_f.rearrange("(a n) -> a n", a=1).to_broadcast((P, DM))).then_inc(s["lnf_in"], 16)

            def load_x(i):
                sp.dma_start(m.gx[i % 4][0:rows(i), :], io.mid[i * P:i * P + rows(i), :]).then_inc(s[f"g_x{i % 4}"], 16)

            load_x(0)
            load_x(1)
            for phase, n, at, _, _ in ph_pairs:
                first = 1 if phase == 0 else 0
                with sp.Fori(first, n) as p:
                    for r in range(2):
                        sp.wait_ge(s["w_lo"], p * 2 + 2 * at + r + 1)
                        load_ffn_weights(sp, s, m, io, phase, p, r)
            for g in range(KT):
                sp.wait_ge(s["w_lo"], 2 * ROUNDS + g + 1)
                load_ffn_weights(sp, s, m, io, len(PAIRS), g // 2, g % 2)
            sp.wait_ge(s["a_lo"], 3 * NE + 3)
            load_x(2)
            load_x(3)
            for i in range(NT):
                sp.wait_ge(s["g_y"], i + 1)
                sp.dma_start(io.yp[i * P:(i + 1) * P, :] if i < TP else io.ys, m.gx[i % 4][0:rows(i), :]
                             ).then_inc(s[f"y_out{i % 4}"], 16)
                if i >= 1 and i + 3 < NT:
                    sp.wait_ge(s[f"y_out{(i - 1) % 4}"], 16 * ((i - 1) // 4 + 1))
                    load_x(i + 3)
            for k in range(4):
                sp.wait_ge(s[f"y_out{k}"], 16 * len(range(k, NT, 4)))

        @block.tensor
        def _(pe):
            for phase, n, at, is_e, e_before in ph_pairs:
                nf = PARTS[phase // 2][1]
                with pe.Fori(0, n) as p:
                    for r in range(2):
                        pe.wait_ge(s["w_lo"], p * 2 + 2 * at + r + 3)
                        for q in range(3):
                            if r == 1:
                                pe.wait_ge(s["odd_drained"], p * 3 + 3 * at + q + 1)
                            elif is_e:
                                pe.wait_ge(s["gate_drained"], p * 3 + 3 * e_before + q + 1)
                                pe.wait_ge(s["y_drained"], 3 * (at - e_before) + 3)
                            else:
                                pe.wait_ge(s["y_drained"], p * 3 + 3 * (at - e_before) + q + 1)
                                pe.wait_ge(s["gate_drained"], 3 * e_before + 3)
                            if not is_e:
                                pe.wait_ge(s["a_lo"], 3 * e_before + q + 1)
                            count = KT if is_e else nf
                            src = m.h2T if is_e else m.aT
                            for k in range(count):
                                last = split_products(pe, m.banks[:, 3 * r + q, 0:TC],
                                                      [w[:, P * k:P * k + P] for w in m.wring[r]],
                                                      [x[:, k, tok[q]] for x in src], k == 0, k == count - 1)
                            last.then_inc(s["f_mm"], 1)

            pe.wait_ge(s["gate_drained"], 3 * NE + 3)
            pe.wait_ge(s["odd_drained"], 3 * ROUNDS + 3)
            pe.wait_ge(s["a_lo"], 3 * NE + 3)

            def products(j, n):
                i = KT * j + n
                lo, hi = group_tok[j]
                pe.wait_ge(s["w_lo"], 2 * ROUNDS + n + 3)
                wait(pe, "y_done", i - 3)
                nf = PARTS[-1][1]
                for f in range(nf):
                    last = split_products(pe, m.banks[:, i % 4, 0:hi - lo], [w[:, P * f:P * f + P] for w in m.wlast[n]],
                                          [x[:, f, lo:hi] for x in m.aT], f == 0, f == nf - 1)
                last.then_inc(s["l_mm"], 1)

            def tile(t):
                j = [t in range(*g) for g in GROUPS].index(True)
                r = rows(t)
                pe.wait_ge(s["y_done"], KT * (j + 1))
                wait(pe, "g_sum", t - 1)
                for k in range(KT):
                    last = pe.transpose(m.banks[0:r, 4 + 2 * (t % 2) + k // 4, P * (k % 4):P * (k % 4) + P],
                                        m.yT[:, k, t * P:t * P + r], m.ident)
                last.then_inc(s["g_turned"], 1)

            last_order(products, tile)

        @block.scalar
        def _(act):
            own = Links(act, s, "own_act")

            act.sem_inc(s["gate_drained"], 3)

            def split(r, g_in, slot):
                act.wait_ge(s[f"ffw_in{r}"], g_in)
                round_to_hi(act, slot[0], m.wstage[r]).then_inc(s["w_hi"], 1)

            for r in range(2):
                split(r, 16, m.wring[r])
            for phase, n, at, is_e, e_before in ph_pairs:
                with act.Fori(0, n) as p:
                    if is_e:
                        for q in range(3):
                            act.wait_ge(s["f_mm"], p * 6 + 6 * at + q + 1)
                            act.wait_ge(s["a_lo"], p * 3 + 3 * e_before + q + 1)
                            act.activation(m.sg[q], m.banks[:, q, 0:TC], ACT.Silu).then_inc(s["gate_drained"], 1)
                    for r in range(2):
                        act.wait_ge(s["f_mm"], p * 6 + 6 * at + 3 * r + 3)
                        split(r, p * 16 + 16 * at + 32, m.wring[r])
            act.wait_ge(s["f_mm"], 6 * ROUNDS)
            for g in range(2, KT):
                split(g % 2, 16 * (ROUNDS + g // 2 + 1), m.wlast[g])
            act.wait_ge(s["w_lo"], 2 * ROUNDS + KT + 2)
            for i in range(NT):
                r = rows(i)
                act.wait_ge(s["g_sum"], i + 1)
                own.after(act.activation(m.gsq[0:r, :], m.gx[i % 4][0:r, :], ACT.Square, accum_out=m.small[0:r, i:i + 1]))
                act.activation(m.small[0:r, 16 + i:17 + i], m.small[0:r, i:i + 1], ACT.Sqrt,
                               bias=m.small[0:r, 64:65], scale=1.0 / DM).then_inc(s["g_rms"], 1)

        @block.gpsimd
        def _(pool):
            pool.sem_inc(s["w_lo"], 2)
            pool.sem_inc(s["a_lo"], 3)

            def split(r, hi_count, slot):
                pool.wait_ge(s["w_hi"], hi_count)
                rest_to_lo(pool, slot[1], m.wstage[r], slot[0]).then_inc(s["w_lo"], 1)

            for r in range(2):
                split(r, r + 1, m.wring[r])
            for phase, n, at, is_e, e_before in ph_pairs:
                with pool.Fori(0, n) as p:
                    split(0, p * 2 + 2 * at + 3, m.wring[0])
                    if is_e:
                        for q in range(3):
                            pool.wait_ge(s["a_hi"], p * 3 + 3 * e_before + q + 1)
                            hi, lo = (x[:, bass.ds(p, 1), tok[q]].rearrange("p f t -> p (f t)") for x in m.aT)
                            rest_to_lo(pool, lo, m.sg[q], hi).then_inc(s["a_lo"], 1)
                    split(1, p * 2 + 2 * at + 4, m.wring[1])
            for g in range(2, KT):
                split(g % 2, 2 * ROUNDS + g + 1, m.wlast[g])

        @block.vector
        def _(dve):
            own = Links(dve, s, "own_dve")
            dve.sem_inc(s["y_drained"], 3)
            dve.sem_inc(s["odd_drained"], 3)
            for phase, n, at, is_e, e_before in ph_pairs:
                with dve.Fori(0, n) as p:
                    if is_e:
                        for q in range(3):
                            dve.wait_ge(s["f_mm"], p * 6 + 6 * at + 3 + q + 1)
                            dve.wait_ge(s["gate_drained"], p * 3 + 3 * e_before + q + 4)
                            dve.tensor_tensor(m.sg[q], m.banks[:, 3 + q, 0:TC], m.sg[q], ALU.mult
                                              ).then_inc(s["odd_drained"], 1)
                            dve.wait_ge(s["odd_drained"], p * 3 + 3 * at + q + 4)
                            hi = m.aT[0][:, bass.ds(p, 1), tok[q]].rearrange("p f t -> p (f t)")
                            dve.tensor_copy(hi, m.sg[q]).then_inc(s["a_hi"], 1)
                    else:
                        for r in range(2):
                            for q in range(3):
                                y = m.yT[:, bass.ds(p * 2 + r, 1), tok[q]].rearrange("p k t -> p (k t)")
                                b = m.banks[:, 3 * r + q, 0:TC]
                                dve.wait_ge(s["f_mm"], p * 6 + 6 * at + 3 * r + q + 1)
                                if phase == 1:
                                    add = dve.tensor_copy(y, b)
                                else:
                                    add = dve.tensor_tensor(y, b, y, ALU.add)
                                add.then_inc(s["y_drained" if r == 0 else "odd_drained"], 1)
            dve.wait_ge(s["lnf_in"], 16)

            def products(j, n):
                i = KT * j + n
                lo, hi = group_tok[j]
                y = m.yT[:, n, lo:hi]
                dve.wait_ge(s["l_mm"], i + 1)
                dve.tensor_tensor(y, m.banks[:, i % 4, 0:hi - lo], y, ALU.add).then_inc(s["y_done"], 1)

            def scaled(t):
                r = rows(t)
                x = m.gx[t % 4][0:r, :]
                dve.wait_ge(s["g_rms"], t + 1)
                own.after(dve.reciprocal(m.small[0:r, 32 + t:33 + t], m.small[0:r, 16 + t:17 + t]))
                dve.scalar_tensor_tensor(out=x, in0=x, scalar=m.small[0:r, 32 + t:33 + t], in1=m.lnb[0:r, :],
                                         op0=ALU.mult, op1=ALU.mult).then_inc(s["g_y"], 1)

            def tile(t):
                r = rows(t)
                dve.wait_ge(s[f"g_x{t % 4}"], 16 * (t // 4 + 1))
                dve.wait_ge(s["g_turned"], t + 1)
                b = m.banks[0:r, 4 + 2 * (t % 2):6 + 2 * (t % 2), :].rearrange("p a n -> p (a n)")
                dve.tensor_tensor(m.gx[t % 4][0:r, :], b, m.gx[t % 4][0:r, :], ALU.add).then_inc(s["g_sum"], 1)
                if t:
                    scaled(t - 1)

            last_order(products, tile)
            scaled(NT - 1)

def build(nc, x_prompt, x_sample, cache_kv, cache_win, state_ret, page_table, ln1, w_in, cmp_pos_k, cmp_w1_k,
          cmp_w2_k, cmp_pos_v, cmp_w1_v, cmp_w2_v, w_out, ln2, w_gate, w_up, w_down, ln_f, const,
          y_prompt, y_sample, kv_prompt, kv_sample, win_prompt, win_sample, ret_prompt, ret_sample):
    io = Named()
    io.xp, io.xs = x_prompt[0], x_sample.rearrange("b s d -> (b s) d")
    io.const, io.ln1, io.ln2, io.ln_f = const, ln1, ln2, ln_f
    io.w_in = w_in[0].rearrange("(k p) n -> p k n", p=P)
    io.pool = cache_kv[0].rearrange("n (c t) s g d -> n c t (s g d)", t=CH)
    io.kvp = kv_prompt[0, 0].rearrange("t s g d -> t (s g d)")
    io.kvs = kv_sample[0].rearrange("b t s g d -> (b t) (s g d)")
    io.winp = win_prompt[0, 0].rearrange("t s g d -> t (s g d)")
    io.cwin = cache_win[0].rearrange("b t s g d -> b t (s g d)")
    io.wins = win_sample[0].rearrange("b t s g d -> b t (s g d)")
    io.retp = ret_prompt[0, 0].rearrange("(a h) d e -> a (h d) e", h=2)
    io.state_in = state_ret[0].rearrange("b h d e -> (b h) (d e)")
    io.state_out = ret_sample[0].rearrange("b h d e -> (b h) (d e)")
    io.table = page_table.rearrange("b n -> (b n)").rearrange("(a n) -> a n", a=1)
    io.w1 = [w[0].rearrange("(k p) n -> p k n", p=P) for w in (cmp_w1_k, cmp_w1_v)]
    io.w2 = [w[0].rearrange("(m p) n -> p m n", p=P) for w in (cmp_w2_k, cmp_w2_v)]
    io.pos = [w[0].rearrange("(k t) d -> (t d) k", t=2) for w in (cmp_pos_k, cmp_pos_v)]
    io.w_out = w_out[0]
    io.w_gate, io.w_up = (w[0].rearrange("(k p) n -> p k n", p=P) for w in (w_gate, w_up))
    io.w_down = w_down[0].rearrange("(f p) n -> p f n", p=P)
    io.yp, io.ys = y_prompt[0], y_sample.rearrange("b s d -> (b s) d")
    io.mid = nc.dram_tensor("mid", (TOK, DM), F32).ap()
    io.gate_rows = nc.dram_tensor("gate_rows", (NB_SEQ, GW), F32).ap()
    io.ret_rows = nc.dram_tensor("ret_rows", (NB_SEQ, 8, 4, HD), F32).ap()
    io.ret_out = nc.dram_tensor("ret_out", (NB_SEQ, 512), F32).ap()
    with ExitStack() as ctx:
        s = Semaphores(nc, ctx)
        m = place_core(nc, ctx)
        with ExitStack() as kept:
            with ExitStack() as hidden:
                place_hidden(nc, hidden, m)
                with ExitStack() as part:
                    place_retention(nc, part, m)
                    stage_project(nc, s, m, io, 0, 4)
                place_kept(nc, kept, m)
                with ExitStack() as part:
                    place_keys(nc, part, m)
                    stage_project(nc, s, m, io, 4, NCH)
            place_mixer(nc, kept, m)
            stage_sequences(nc, s, m, io)
            stage_attention(nc, s, m, io)
        place_feed_forward(nc, ctx, m)
        stage_mix_out(nc, s, m, io)
        stage_feed_forward(nc, s, m, io)

_INS = ['x_prompt', 'x_sample', 'cache_kv', 'cache_win', 'state_ret', 'page_table', 'ln1', 'w_in', 'cmp_pos_k',
        'cmp_w1_k', 'cmp_w2_k', 'cmp_pos_v', 'cmp_w1_v', 'cmp_w2_v', 'w_out', 'ln2', 'w_gate', 'w_up', 'w_down',
        'ln_f']
_OUTS = [(1, SEQ, DM), (NB_SEQ, 1, DM), (1, 1, SEQ, 4, 2, HD), (1, NB_SEQ, 1, 4, 2, HD), (1, 1, WIN, 2, 2, HD),
         (1, NB_SEQ, WIN, 2, 2, HD), (1, 1, 8, HD, HD), (1, NB_SEQ, 8, HD, HD)]


def kernel(**inputs):
    import concourse.bacc as bacc
    from concourse.bass_utils import run_bass_kernel_spmd as run

    arrays = {f"in_{n}": np.ascontiguousarray(inputs[n]) for n in _INS}
    arrays["in_const"] = constants()
    nc = bacc.Bacc("TRN2", target_bir_lowering=False, num_devices=1)
    args = [nc.dram_tensor(n, a.shape, mybir.dt.from_np(a.dtype), kind="ExternalInput").ap() for n, a in arrays.items()]
    args += [nc.dram_tensor(f"out_{i}", s, F32, kind="ExternalOutput").ap() for i, s in enumerate(_OUTS)]
    build(nc, *args)
    r = run(nc, [arrays], core_ids=[0])
    return tuple(r.results[0][f"out_{i}"] for i in range(len(_OUTS)))
```
